# Optimizing a Trainium2 kernel written in Bass

```python
import math
import jax, jax.numpy as jnp
from jax import lax
import numpy as np

D_MODEL = 1024
BATCH = 1
SEQ = 512
DEPTH = 2

MEM_LEN = 256
DA_HEADS = 8
DA_HEAD_DIM = 64
DA_V_DIM = 2 * DA_HEAD_DIM
DA_WIDTH = DA_HEADS * DA_V_DIM
QK_WIDTH = DA_HEADS * 2 * DA_HEAD_DIM
LAMBDA_INIT_SCALE = 0.1
CONV_WIDTH = 512
CONV_K = 3
MEM_HEADS = 4
MEM_HEAD_DIM = 128
MEM_WIDTH = MEM_HEADS * MEM_HEAD_DIM
N_BRANCH = 3
ROPE_THETA = 10000.0
Q_BLOCK = 128
N_EXPERTS = 16
N_GROUPS = 4
EXPERTS_PER_GROUP = N_EXPERTS // N_GROUPS
TOP_K = 2
D_FF_EXPERT = 512
EXPERT_BLOCK = 128
LN_EPS = 1e-5
RMS_EPS = 1e-5
DEEPNORM_ALPHA = (2 * DEPTH) ** 0.25
DEEPNORM_BETA = (8 * DEPTH) ** -0.25

IN_SIZES = (QK_WIDTH, QK_WIDTH, DA_WIDTH, CONV_WIDTH, CONV_WIDTH, CONV_WIDTH, MEM_WIDTH, N_BRANCH * D_MODEL)
IN_COLS = sum(IN_SIZES)
IN_SPLITS = tuple(sum(IN_SIZES[:i + 1]) for i in range(len(IN_SIZES) - 1))


def layer_norm(x, g, b):
    x32 = x.astype(jnp.float32)
    mu = jnp.mean(x32, axis=-1, keepdims=True)
    var = jnp.mean(jnp.square(x32 - mu), axis=-1, keepdims=True)
    y = (x32 - mu) * lax.rsqrt(var + LN_EPS) * g.astype(jnp.float32) + b.astype(jnp.float32)
    return y.astype(x.dtype)

def rope(t, cos, sin):
    half = t.shape[-1] // 2
    t1, t2 = t[..., :half], t[..., half:]
    cos = cos.astype(t.dtype)
    sin = sin.astype(t.dtype)
    return jnp.concatenate([t1 * cos - t2 * sin, t2 * cos + t1 * sin], axis=-1)

def diff_attention(q, k, v, lam, lam_init, subln_g):
    B, S = q.shape[0], q.shape[1]
    qh = jnp.transpose(q, (0, 2, 3, 1, 4))
    kh = jnp.transpose(k, (0, 2, 3, 1, 4))
    vh = jnp.transpose(v, (0, 2, 1, 3))
    scale = DA_HEAD_DIM ** -0.5
    outs = []
    for blk in range(S // Q_BLOCK):
        s0 = blk * Q_BLOCK
        end = s0 + Q_BLOCK
        qb = qh[:, :, :, s0:end]
        kb = kh[:, :, :, :end]
        sc = jnp.einsum('bhcqd,bhckd->bhcqk', qb, kb).astype(jnp.float32) * scale
        causal = jnp.arange(end)[None, :] <= (s0 + jnp.arange(Q_BLOCK))[:, None]
        sc = jnp.where(causal, sc, -jnp.inf)
        p = jax.nn.softmax(sc, axis=-1)
        a = p[:, :, 0] - lam * p[:, :, 1]
        outs.append(jnp.einsum('bhqk,bhkd->bhqd', a.astype(v.dtype), vh[:, :, :end]))
    o = jnp.concatenate(outs, axis=2).astype(jnp.float32)
    o = o * lax.rsqrt(jnp.mean(jnp.square(o), axis=-1, keepdims=True) + RMS_EPS)
    o = o * subln_g.astype(jnp.float32) * (1.0 - lam_init)
    o = jnp.transpose(o, (0, 2, 1, 3)).astype(v.dtype)
    return o.reshape(B, S, DA_WIDTH)

def short_gated_conv(bg, cg, u, w):
    z = cg * u
    S = z.shape[1]
    zp = jnp.pad(z, ((0, 0), (CONV_K - 1, 0), (0, 0)))
    y = w[0] * zp[:, 0:S]
    for tap in range(1, CONV_K):
        y = y + w[tap] * zp[:, tap:tap + S]
    return bg * y

def memory_attention(qm, mem, w_kv):
    B, S = qm.shape[0], qm.shape[1]
    M = mem.shape[1]
    kv = mem @ w_kv
    km = kv[..., :MEM_WIDTH].reshape(B, M, MEM_HEADS, MEM_HEAD_DIM)
    vm = kv[..., MEM_WIDTH:].reshape(B, M, MEM_HEADS, MEM_HEAD_DIM)
    q = qm.reshape(B, S, MEM_HEADS, MEM_HEAD_DIM)
    sc = jnp.einsum('bshd,bmhd->bhsm', q, km).astype(jnp.float32) * (MEM_HEAD_DIM ** -0.5)
    p = jax.nn.softmax(sc, axis=-1)
    o = jnp.einsum('bhsm,bmhd->bshd', p.astype(vm.dtype), vm)
    return o.reshape(B, S, MEM_WIDTH)

def grouped_moe(x2d, w_router, router_bias, w_gate, w_up, w_down):
    T, D = x2d.shape
    logits = (x2d @ w_router).astype(jnp.float32) + router_bias.astype(jnp.float32)
    scores = jax.nn.softmax(logits, axis=-1)
    grouped = scores.reshape(T, N_GROUPS, EXPERTS_PER_GROUP)
    g_idx = jnp.argmax(jnp.max(grouped, axis=-1), axis=-1)
    in_group = jnp.take_along_axis(grouped, g_idx[:, None, None], axis=1)[:, 0]
    top_vals, top_idx = lax.top_k(in_group, TOP_K)
    experts = g_idx[:, None] * EXPERTS_PER_GROUP + top_idx
    weights = top_vals / jnp.sum(top_vals, axis=-1, keepdims=True)

    A = T * TOP_K
    e_flat = experts.reshape(A).astype(jnp.int32)
    tok_flat = jnp.repeat(jnp.arange(T, dtype=jnp.int32), TOP_K)
    gate_flat = weights.reshape(A).astype(x2d.dtype)
    order = jnp.argsort(e_flat)
    e_sorted = e_flat[order]
    counts = jnp.zeros((N_EXPERTS,), jnp.int32).at[e_flat].add(1)
    start = jnp.cumsum(counts) - counts
    padded = ((counts + EXPERT_BLOCK - 1) // EXPERT_BLOCK) * EXPERT_BLOCK
    pad_end = jnp.cumsum(padded)
    pad_start = pad_end - padded
    dest = pad_start[e_sorted] + (jnp.arange(A, dtype=jnp.int32) - start[e_sorted])
    P = ((A + EXPERT_BLOCK - 1) // EXPERT_BLOCK) * EXPERT_BLOCK + N_EXPERTS * EXPERT_BLOCK
    n_blocks = P // EXPERT_BLOCK
    buf_tok = jnp.full((P,), T, jnp.int32).at[dest].set(tok_flat[order])
    buf_gate = jnp.zeros((P,), x2d.dtype).at[dest].set(gate_flat[order])
    blk_start = jnp.arange(n_blocks, dtype=jnp.int32) * EXPERT_BLOCK
    blk_expert = jnp.minimum(jnp.searchsorted(pad_end, blk_start, side='right'), N_EXPERTS - 1).astype(jnp.int32)
    x_pad = jnp.concatenate([x2d, jnp.zeros((1, D), x2d.dtype)], axis=0)
    xb = x_pad[buf_tok].reshape(n_blocks, EXPERT_BLOCK, D)

    def expert_block(args):
        xblk, e = args
        h = jax.nn.silu(xblk @ w_gate[e]) * (xblk @ w_up[e])
        return h @ w_down[e]

    yb = lax.map(expert_block, (xb, blk_expert))
    y = yb.reshape(P, D) * buf_gate[:, None]
    return jax.ops.segment_sum(y, buf_tok, num_segments=T + 1)[:T]

def first_inputs(seed: int = 0) -> dict:
    key = jax.random.key(seed)
    ks = jax.random.split(key, 26)
    f32 = jnp.float32

    def nrm(k, shape, fan_in, scale=1.0):
        return jax.random.normal(k, shape, f32) * (scale * fan_in ** -0.5)

    x = jax.random.normal(ks[0], (BATCH, SEQ, D_MODEL), f32)
    mem = jax.random.normal(ks[1], (BATCH, MEM_LEN, D_MODEL), f32)
    positions = (jax.random.randint(ks[2], (BATCH, 1), 0, 4096, jnp.int32)
                 + jnp.arange(SEQ, dtype=jnp.int32)[None, :])
    col_scale = jnp.concatenate([
        jnp.ones((2 * QK_WIDTH,), f32),
        jnp.full((DA_WIDTH,), DEEPNORM_BETA, f32),
        jnp.ones((IN_COLS - 2 * QK_WIDTH - DA_WIDTH,), f32)])
    w_in = nrm(ks[3], (DEPTH, D_MODEL, IN_COLS), D_MODEL) * col_scale
    lambda_q1 = LAMBDA_INIT_SCALE * jax.random.normal(ks[4], (DEPTH, DA_HEAD_DIM), f32)
    lambda_k1 = LAMBDA_INIT_SCALE * jax.random.normal(ks[5], (DEPTH, DA_HEAD_DIM), f32)
    lambda_q2 = LAMBDA_INIT_SCALE * jax.random.normal(ks[6], (DEPTH, DA_HEAD_DIM), f32)
    lambda_k2 = LAMBDA_INIT_SCALE * jax.random.normal(ks[7], (DEPTH, DA_HEAD_DIM), f32)
    diff_subln_g = 1.0 + 0.02 * jax.random.normal(ks[8], (DEPTH, DA_V_DIM), f32)
    conv_w = nrm(ks[9], (DEPTH, CONV_K, CONV_WIDTH), CONV_K)
    w_mem_kv = nrm(ks[10], (DEPTH, D_MODEL, 2 * MEM_WIDTH), D_MODEL)
    w_br_attn = nrm(ks[11], (DEPTH, DA_WIDTH, D_MODEL), DA_WIDTH, DEEPNORM_BETA)
    w_br_conv = nrm(ks[12], (DEPTH, CONV_WIDTH, D_MODEL), CONV_WIDTH, DEEPNORM_BETA)
    w_br_mem = nrm(ks[13], (DEPTH, MEM_WIDTH, D_MODEL), MEM_WIDTH, DEEPNORM_BETA)
    w_out = nrm(ks[14], (DEPTH, D_MODEL, D_MODEL), D_MODEL, DEEPNORM_BETA)
    ln1_g = 1.0 + 0.02 * jax.random.normal(ks[15], (DEPTH, D_MODEL), f32)
    ln1_b = 0.02 * jax.random.normal(ks[16], (DEPTH, D_MODEL), f32)
    ln2_g = 1.0 + 0.02 * jax.random.normal(ks[17], (DEPTH, D_MODEL), f32)
    ln2_b = 0.02 * jax.random.normal(ks[18], (DEPTH, D_MODEL), f32)
    w_router = nrm(ks[19], (D_MODEL, N_EXPERTS), D_MODEL)
    router_bias = 0.01 * jax.random.normal(ks[20], (N_EXPERTS,), f32)
    w_exp_gate = nrm(ks[21], (DEPTH, N_EXPERTS, D_MODEL, D_FF_EXPERT), D_MODEL, DEEPNORM_BETA)
    w_exp_up = nrm(ks[22], (DEPTH, N_EXPERTS, D_MODEL, D_FF_EXPERT), D_MODEL, DEEPNORM_BETA)
    w_exp_down = nrm(ks[23], (DEPTH, N_EXPERTS, D_FF_EXPERT, D_MODEL), D_FF_EXPERT, DEEPNORM_BETA)
    return {'x': x, 'mem': mem, 'positions': positions, 'w_in': w_in,
            'lambda_q1': lambda_q1, 'lambda_k1': lambda_k1, 'lambda_q2': lambda_q2, 'lambda_k2': lambda_k2,
            'diff_subln_g': diff_subln_g, 'conv_w': conv_w, 'w_mem_kv': w_mem_kv,
            'w_br_attn': w_br_attn, 'w_br_conv': w_br_conv, 'w_br_mem': w_br_mem, 'w_out': w_out,
            'ln1_g': ln1_g, 'ln1_b': ln1_b, 'ln2_g': ln2_g, 'ln2_b': ln2_b,
            'w_router': w_router, 'router_bias': router_bias,
            'w_exp_gate': w_exp_gate, 'w_exp_up': w_exp_up, 'w_exp_down': w_exp_down}

def first_block(x, mem, positions, w_in, lambda_q1, lambda_k1, lambda_q2, lambda_k2, diff_subln_g,
              conv_w, w_mem_kv, w_br_attn, w_br_conv, w_br_mem, w_out,
              ln1_g, ln1_b, ln2_g, ln2_b, w_router, router_bias,
              w_exp_gate, w_exp_up, w_exp_down):
    B, S, D = x.shape
    inv_freq = ROPE_THETA ** (-jnp.arange(0, DA_HEAD_DIM, 2, dtype=jnp.float32) / DA_HEAD_DIM)
    ang = positions.astype(jnp.float32)[..., None] * inv_freq
    cos = jnp.cos(ang)[:, :, None, :]
    sin = jnp.sin(ang)[:, :, None, :]

    for l in range(DEPTH):
        lam_init = 0.8 - 0.6 * math.exp(-0.3 * l)
        proj = x @ w_in[l]
        q, k, v, cb, cc, cu, qm, gates = jnp.split(proj, IN_SIZES and IN_SPLITS, axis=-1)

        q = rope(q.reshape(B, S, DA_HEADS * 2, DA_HEAD_DIM), cos, sin).reshape(B, S, DA_HEADS, 2, DA_HEAD_DIM)
        k = rope(k.reshape(B, S, DA_HEADS * 2, DA_HEAD_DIM), cos, sin).reshape(B, S, DA_HEADS, 2, DA_HEAD_DIM)
        v = v.reshape(B, S, DA_HEADS, DA_V_DIM)
        lam = (jnp.exp(jnp.sum(lambda_q1[l].astype(jnp.float32) * lambda_k1[l].astype(jnp.float32)))
               - jnp.exp(jnp.sum(lambda_q2[l].astype(jnp.float32) * lambda_k2[l].astype(jnp.float32)))
               + lam_init)
        y_attn = diff_attention(q, k, v, lam, lam_init, diff_subln_g[l])

        y_conv = short_gated_conv(cb, cc, cu, conv_w[l])

        y_mem = memory_attention(qm, mem, w_mem_kv[l])

        g = jax.nn.sigmoid(gates.reshape(B, S, N_BRANCH, D))
        merged = (g[:, :, 0] * (y_attn @ w_br_attn[l])
                  + g[:, :, 1] * (y_conv @ w_br_conv[l])
                  + g[:, :, 2] * (y_mem @ w_br_mem[l]))
        mix = merged @ w_out[l]
        x = layer_norm(DEEPNORM_ALPHA * x + mix, ln1_g[l], ln1_b[l])

        f = grouped_moe(x.reshape(B * S, D), w_router, router_bias,
                        w_exp_gate[l], w_exp_up[l], w_exp_down[l]).reshape(B, S, D)
        x = layer_norm(DEEPNORM_ALPHA * x + f, ln2_g[l], ln2_b[l])
    return x


DEPTH_2 = 1

RWKV_WIDTH = D_MODEL // 2
RWKV_HEAD = 64
RWKV_HEADS = RWKV_WIDTH // RWKV_HEAD
DECAY_RANK = 64
AAA_RANK = 64
GATE_RANK = 128
RWKV_SPLITS = (RWKV_WIDTH, 2 * RWKV_WIDTH, 3 * RWKV_WIDTH,
               3 * RWKV_WIDTH + DECAY_RANK, 3 * RWKV_WIDTH + DECAY_RANK + AAA_RANK)
N_RWKV_COLS = 3 * RWKV_WIDTH + DECAY_RANK + AAA_RANK + GATE_RANK
LNX_EPS = 64e-5
S5_WIDTH = D_MODEL // 2
S5_GROUP = 16
S5_GROUPS = S5_WIDTH // S5_GROUP
S5_STATE = 64
STEP_MIN = 1e-3
STEP_MAX = 1e-1
N_IN_COLS = N_RWKV_COLS + S5_WIDTH + 2 * D_MODEL
D_FF = 256 * ((8 * D_MODEL // 3 + 255) // 256)
CONV_WIDTH_2 = 3
NORM_EPS = 1e-6


def rms_norm(x, g):
    xf = x.astype(jnp.float32)
    y = xf * lax.rsqrt(jnp.mean(xf * xf, axis=-1, keepdims=True) + NORM_EPS)
    return y.astype(x.dtype) * g

def token_shift(p, mu):
    prev = jnp.pad(p, ((0, 0), (1, 0), (0, 0)))[:, :-1]
    return p + (prev - p) * mu

def wkv7_scan(r, decay, k, v, a_vec, b_vec):
    bsz, _, nh, n = r.shape

    def step(S, inp):
        r_t, w_t, k_t, v_t, a_t, b_t = inp
        sa = jnp.einsum('bhij,bhj->bhi', S, a_t)
        S = (S * w_t[:, :, None, :] + sa[..., None] * b_t[:, :, None, :]
             + v_t[..., None] * k_t[:, :, None, :])
        return S, jnp.einsum('bhij,bhj->bhi', S, r_t)

    xs = tuple(jnp.moveaxis(t, 1, 0) for t in (r, decay, k, v, a_vec, b_vec))
    S0 = jnp.zeros((bsz, nh, n, n), jnp.float32)
    _, ys = lax.scan(step, S0, xs)
    return jnp.moveaxis(ys, 0, 1)

def rwkv7_branch(p, mu, w0, w2, a0, a2, g2, k_k, k_a, r_k, lnx_w, lnx_b):
    dtype = p.dtype
    f32 = jnp.float32
    bsz, L, _ = p.shape
    p = token_shift(p.astype(f32), mu.astype(f32))
    r, k, v, wd, ad, gd = jnp.split(p, RWKV_SPLITS, axis=-1)
    w = -jax.nn.softplus(-(w0 + jnp.tanh(wd) @ w2)) - 0.5
    decay = jnp.exp(-jnp.exp(w))
    a = jax.nn.sigmoid(a0 + ad @ a2)
    g = jax.nn.sigmoid(gd) @ g2
    hs = (bsz, L, RWKV_HEADS, RWKV_HEAD)
    kk = (k * k_k).reshape(hs)
    kk = kk / jnp.maximum(jnp.linalg.norm(kk, axis=-1, keepdims=True), 1e-12)
    k = k * (1.0 + (a - 1.0) * k_a)
    rh, kh, vh = r.reshape(hs), k.reshape(hs), v.reshape(hs)
    ah = a.reshape(hs)
    y = wkv7_scan(rh, decay.reshape(hs), kh, vh, -kk, kk * ah)
    mean = jnp.mean(y, axis=-1, keepdims=True)
    var = jnp.mean(jnp.square(y - mean), axis=-1, keepdims=True)
    y = ((y - mean) * lax.rsqrt(var + LNX_EPS)).reshape(bsz, L, RWKV_WIDTH) * lnx_w + lnx_b
    bonus = jnp.sum(rh * kh * r_k, axis=-1, keepdims=True) * vh
    y = (y + bonus.reshape(bsz, L, RWKV_WIDTH)) * g
    return y.astype(dtype)

def s5_combine(left, right):
    a_i, b_i = left
    a_j, b_j = right
    return a_j * a_i, a_j * b_i + b_j

def s5_branch(u, a_re, a_im, b_re, b_im, c_re, c_im, d, log_step, w_glu, b_glu):
    f32 = jnp.float32
    bsz, L, _ = u.shape
    lam = lax.complex(a_re.astype(f32), a_im.astype(f32))
    dt = jnp.exp(log_step.astype(f32))[:, None]
    a_bar = jnp.exp(lam * dt)
    b_bar = ((a_bar - 1.0) / lam)[..., None] * lax.complex(b_re.astype(f32), b_im.astype(f32))
    c = lax.complex(c_re.astype(f32), c_im.astype(f32))
    ug = u.astype(f32).reshape(bsz, L, S5_GROUPS, S5_GROUP)
    bu = jnp.einsum('gpc,blgc->blgp', b_bar, ug.astype(jnp.complex64))
    a_elems = jnp.broadcast_to(a_bar, (1, L, S5_GROUPS, S5_STATE))
    _, states = lax.associative_scan(s5_combine, (a_elems, bu), axis=1)
    y = jnp.real(jnp.einsum('gcp,blgp->blgc', c, states)) + d.astype(f32).reshape(S5_GROUPS, S5_GROUP) * ug
    y = jax.nn.gelu(y.reshape(bsz, L, S5_WIDTH)).astype(u.dtype)
    return y * jax.nn.sigmoid(y @ w_glu + b_glu)

def conv_ffn(h, w_up, conv_w, conv_b, w_down):
    L = h.shape[1]
    z = h @ w_up
    zp = jnp.pad(z, ((0, 0), (CONV_WIDTH_2 - 1, 0), (0, 0)))
    z = conv_b + sum(conv_w[j] * zp[:, j:j + L] for j in range(CONV_WIDTH_2))
    gate, val = jnp.split(z, 2, axis=-1)
    return (jax.nn.gelu(gate) * val) @ w_down

def second_inputs(seed: int = 0) -> dict:
    key = jax.random.key(seed)
    ks = jax.random.split(key, 40)
    f32 = jnp.float32
    Ld, W, G, P, C, F = DEPTH_2, RWKV_WIDTH, S5_GROUPS, S5_STATE, S5_GROUP, D_FF

    def nrm(k, shape, scale):
        return jax.random.normal(k, shape, f32) * scale

    def gain(k, shape):
        return 1.0 + 0.05 * jax.random.normal(k, shape, f32)

    n = jnp.arange(P, dtype=f32)
    return {
        'x': nrm(ks[0], (BATCH, SEQ, D_MODEL), 1.0),
        'norm_mix_pre': gain(ks[1], (Ld, D_MODEL)),
        'norm_mix_post': gain(ks[2], (Ld, D_MODEL)),
        'norm_ffn_pre': gain(ks[3], (Ld, D_MODEL)),
        'norm_ffn_post': gain(ks[4], (Ld, D_MODEL)),
        'w_in': nrm(ks[5], (Ld, D_MODEL, N_IN_COLS), D_MODEL ** -0.5),
        'b_gate': nrm(ks[6], (Ld, 2 * D_MODEL), 0.02),
        'rwkv_shift_mu': jax.random.uniform(ks[7], (Ld, N_RWKV_COLS), f32, 0.0, 1.0),
        'rwkv_w0': jax.random.uniform(ks[8], (Ld, W), f32, -6.0, -1.0),
        'rwkv_w2': nrm(ks[9], (Ld, DECAY_RANK, W), 0.1 * DECAY_RANK ** -0.5),
        'rwkv_a0': nrm(ks[10], (Ld, W), 0.1),
        'rwkv_a2': nrm(ks[11], (Ld, AAA_RANK, W), 0.1 * AAA_RANK ** -0.5),
        'rwkv_g2': nrm(ks[12], (Ld, GATE_RANK, W), GATE_RANK ** -0.5),
        'rwkv_k_k': 0.85 + 0.05 * jax.random.normal(ks[13], (Ld, W), f32),
        'rwkv_k_a': gain(ks[14], (Ld, W)),
        'rwkv_r_k': nrm(ks[15], (Ld, RWKV_HEADS, RWKV_HEAD), 0.3),
        'rwkv_lnx_w': gain(ks[16], (Ld, W)),
        'rwkv_lnx_b': nrm(ks[17], (Ld, W), 0.02),
        's5_a_re': -0.5 + 0.01 * jax.random.normal(ks[18], (Ld, G, P), f32),
        's5_a_im': math.pi * n + 0.01 * jax.random.normal(ks[19], (Ld, G, P), f32),
        's5_b_re': nrm(ks[20], (Ld, G, P, C), (2 * C) ** -0.5),
        's5_b_im': nrm(ks[21], (Ld, G, P, C), (2 * C) ** -0.5),
        's5_c_re': nrm(ks[22], (Ld, G, C, P), P ** -0.5),
        's5_c_im': nrm(ks[23], (Ld, G, C, P), P ** -0.5),
        's5_d': nrm(ks[24], (Ld, S5_WIDTH), 1.0),
        's5_log_step': jax.random.uniform(ks[25], (Ld, G), f32, math.log(STEP_MIN), math.log(STEP_MAX)),
        's5_w_glu': nrm(ks[26], (Ld, S5_WIDTH, S5_WIDTH), S5_WIDTH ** -0.5),
        's5_b_glu': nrm(ks[27], (Ld, S5_WIDTH), 0.02),
        'w_branch_rwkv': nrm(ks[28], (Ld, W, D_MODEL), W ** -0.5),
        'w_branch_s5': nrm(ks[29], (Ld, S5_WIDTH, D_MODEL), S5_WIDTH ** -0.5),
        'w_out': nrm(ks[30], (Ld, D_MODEL, D_MODEL), D_MODEL ** -0.5),
        'ffn_w_up': nrm(ks[31], (Ld, D_MODEL, 2 * F), D_MODEL ** -0.5),
        'ffn_conv_w': nrm(ks[32], (Ld, CONV_WIDTH_2, 2 * F), CONV_WIDTH_2 ** -0.5),
        'ffn_conv_b': nrm(ks[33], (Ld, 2 * F), 0.02),
        'ffn_w_down': nrm(ks[34], (Ld, F, D_MODEL), F ** -0.5),
    }

def second_block(x, norm_mix_pre, norm_mix_post, norm_ffn_pre, norm_ffn_post, w_in, b_gate,
              rwkv_shift_mu, rwkv_w0, rwkv_w2, rwkv_a0, rwkv_a2, rwkv_g2, rwkv_k_k, rwkv_k_a,
              rwkv_r_k, rwkv_lnx_w, rwkv_lnx_b, s5_a_re, s5_a_im, s5_b_re, s5_b_im, s5_c_re,
              s5_c_im, s5_d, s5_log_step, s5_w_glu, s5_b_glu, w_branch_rwkv, w_branch_s5, w_out,
              ffn_w_up, ffn_conv_w, ffn_conv_b, ffn_w_down):
    for l in range(DEPTH_2):
        h = rms_norm(x, norm_mix_pre[l])
        proj = h @ w_in[l]
        p_rwkv = proj[..., :N_RWKV_COLS]
        u_s5 = proj[..., N_RWKV_COLS:N_RWKV_COLS + S5_WIDTH]
        gates = jax.nn.sigmoid(proj[..., N_RWKV_COLS + S5_WIDTH:] + b_gate[l])
        g_rwkv, g_s5 = jnp.split(gates, 2, axis=-1)
        o_rwkv = rwkv7_branch(p_rwkv, rwkv_shift_mu[l], rwkv_w0[l], rwkv_w2[l], rwkv_a0[l],
                              rwkv_a2[l], rwkv_g2[l], rwkv_k_k[l], rwkv_k_a[l], rwkv_r_k[l],
                              rwkv_lnx_w[l], rwkv_lnx_b[l]) @ w_branch_rwkv[l]
        o_s5 = s5_branch(u_s5, s5_a_re[l], s5_a_im[l], s5_b_re[l], s5_b_im[l], s5_c_re[l],
                         s5_c_im[l], s5_d[l], s5_log_step[l], s5_w_glu[l], s5_b_glu[l]) @ w_branch_s5[l]
        mixed = (g_rwkv * o_rwkv + g_s5 * o_s5) @ w_out[l]
        x = x + rms_norm(mixed, norm_mix_post[l])
        h = rms_norm(x, norm_ffn_pre[l])
        f = conv_ffn(h, ffn_w_up[l], ffn_conv_w[l], ffn_conv_b[l], ffn_w_down[l])
        x = x + rms_norm(f, norm_ffn_post[l])
    return x


def setup_inputs(seed=0):
    out = dict(first_inputs(seed))
    for name, value in second_inputs(seed + 1).items():
        if name != "x":
            out[name + "_2"] = value
    return out


def reference(
    x, mem, positions, w_in, lambda_q1, lambda_k1, lambda_q2, lambda_k2, diff_subln_g, conv_w,
    w_mem_kv, w_br_attn, w_br_conv, w_br_mem, w_out, ln1_g, ln1_b, ln2_g, ln2_b, w_router,
    router_bias, w_exp_gate, w_exp_up, w_exp_down, norm_mix_pre_2, norm_mix_post_2,
    norm_ffn_pre_2, norm_ffn_post_2, w_in_2, b_gate_2, rwkv_shift_mu_2, rwkv_w0_2, rwkv_w2_2,
    rwkv_a0_2, rwkv_a2_2, rwkv_g2_2, rwkv_k_k_2, rwkv_k_a_2, rwkv_r_k_2, rwkv_lnx_w_2,
    rwkv_lnx_b_2, s5_a_re_2, s5_a_im_2, s5_b_re_2, s5_b_im_2, s5_c_re_2, s5_c_im_2, s5_d_2,
    s5_log_step_2, s5_w_glu_2, s5_b_glu_2, w_branch_rwkv_2, w_branch_s5_2, w_out_2, ffn_w_up_2,
    ffn_conv_w_2, ffn_conv_b_2, ffn_w_down_2,
):
    x = first_block(
        x, mem, positions, w_in, lambda_q1, lambda_k1, lambda_q2, lambda_k2, diff_subln_g,
        conv_w, w_mem_kv, w_br_attn, w_br_conv, w_br_mem, w_out, ln1_g, ln1_b, ln2_g, ln2_b,
        w_router, router_bias, w_exp_gate, w_exp_up, w_exp_down,
    )
    return second_block(
        x, norm_mix_pre_2, norm_mix_post_2, norm_ffn_pre_2, norm_ffn_post_2, w_in_2, b_gate_2,
        rwkv_shift_mu_2, rwkv_w0_2, rwkv_w2_2, rwkv_a0_2, rwkv_a2_2, rwkv_g2_2, rwkv_k_k_2,
        rwkv_k_a_2, rwkv_r_k_2, rwkv_lnx_w_2, rwkv_lnx_b_2, s5_a_re_2, s5_a_im_2, s5_b_re_2,
        s5_b_im_2, s5_c_re_2, s5_c_im_2, s5_d_2, s5_log_step_2, s5_w_glu_2, s5_b_glu_2,
        w_branch_rwkv_2, w_branch_s5_2, w_out_2, ffn_w_up_2, ffn_conv_w_2, ffn_conv_b_2,
        ffn_w_down_2,
    )


_drawn_inputs = setup_inputs


def setup_inputs(seed=0):
    import zlib

    import numpy as np

    out = dict(_drawn_inputs(seed))
    spreads = {}
    factors = {'lambda_q1': 5.809,
     'lambda_q2': 4.24,
     'lambda_k2': 4.194,
     'diff_subln_g': 8.0,
     'router_bias': 6.678,
     'b_gate_2': 8.0,
     'rwkv_w2_2': 8.0,
     'rwkv_lnx_b_2': 4.518,
     's5_a_re_2': 200.0,
     's5_b_glu_2': 8.0,
     'ffn_conv_b_2': 3.472,
     's5_a_im_2': 34.576,
     's5_b_re_2': 47.888,
     's5_b_im_2': 47.624,
     's5_c_re_2': 47.864,
     's5_c_im_2': 48.096,
     's5_log_step_2': 37.2}
    for name, (base, spread) in spreads.items():
        noise = np.random.default_rng([zlib.crc32(name.encode()), seed]).standard_normal(out[name].shape)
        drawn = base * np.exp(spread * noise) if base else spread * noise
        out[name] = __import__('jax').numpy.asarray(drawn.astype(out[name].dtype))
    for name, factor in factors.items():
        out[name] = (out[name] * factor).astype(out[name].dtype)
    return out
```

```python
from contextlib import ExitStack, nullcontext
import math

import numpy as np
import concourse.bass as bass
from concourse import mybir

F32 = mybir.dt.float32
I32 = mybir.dt.int32
ALU = mybir.AluOpType
ACT = mybir.ActivationFunctionType
AX = mybir.AxisListType.X

P = 128
SEQ = 512
D = 1024
KT = D // P
TT = SEQ // P
DEPTH = 2
HEADS = 8
MEM = 256
MEM_HEADS = 4
CONV = 512
CT = CONV // P
E_N = 16
G_N = 4
FF_E = 512
N_BLOCKS = (SEQ * 2) // P + E_N
RING = 4
ALPHA = (2 * DEPTH) ** 0.25
LN_EPS = 1e-5
RMS_EPS = 1e-5
D_FF = 2816
FF_T = D_FF // P
MAGIC = 12582912.0
TWO_PI_1, TWO_PI_2, TWO_PI_3 = 6.28125, 0.0019340515136718750, 1.2556659146e-06

CONST_NAMES = ["ident", "ones", "ones_over_d", "head_ones", "rotate", "causal", "earlier",
               "chunk_lower", "chunk_upper", "chunk_upper_incl"]


def constants():
    i = np.arange(P)
    chunk = i // 32
    same = chunk[:, None] == chunk[None, :]
    rot = np.zeros((P, P), np.float32)
    for m in range(P):
        if m % 64 < 32:
            rot[m + 32, m] = -1.0
        else:
            rot[m - 32, m] = 1.0
    tables = {
        "ident": np.eye(P),
        "ones": np.ones((P, P)),
        "ones_over_d": np.full((P, P), 1.0 / D),
        "head_ones": (i[:, None] // 64 == i[None, :] // 64),
        "rotate": rot,
        "causal": np.where(i[None, :] <= i[:, None], 0.0, -1e30),
        "earlier": (i[:, None] < i[None, :]),
        "chunk_lower": same & (i[:, None] > i[None, :]),
        "chunk_upper": same & (i[:, None] < i[None, :]),
        "chunk_upper_incl": same & (i[:, None] <= i[None, :]),
    }
    c = np.stack([tables[n] for n in CONST_NAMES], 1).astype(np.float32)
    t = np.arange(SEQ)
    rows = np.stack([np.broadcast_to(t % 32 != 0, (P, SEQ)), np.broadcast_to(t, (P, SEQ))], 1)
    inv_freq = (10000.0 ** (-np.arange(0, 64, 2) / 64)).astype(np.float32)
    small = np.zeros((P, 64), np.float32)
    small[:, 0] = inv_freq[i % 32]
    small[:, 1:17] = 16 - np.arange(16)
    small[:, 17:21] = 4 - np.arange(4)
    small[:, 24:48] = np.arange(N_BLOCKS) * P
    return c, rows.astype(np.float32), small


INV_FREQ, EXPERT_KEY, GROUP_KEY, BLOCK_START = slice(0, 1), slice(1, 17), slice(17, 21), slice(24, 48)


class Columns:

    def __init__(self, widths):
        self.at, n = {}, 0
        for name, w in widths:
            self.at[name] = (n, n + w)
            n += w
        self.total = n


PARAM_WIDTHS = []
for _l in range(DEPTH):
    PARAM_WIDTHS += [(f"subln{_l}", 1), (f"conv_w{_l}", 3 * CT), (f"ln1_g{_l}", KT), (f"ln1_b{_l}", KT),
                     (f"ln2_g{_l}", KT), (f"ln2_b{_l}", KT)]
PARAM_WIDTHS += [("router_bias", E_N), ("norm_mix_pre", KT), ("norm_mix_post", KT), ("norm_ffn_pre", KT),
                 ("norm_ffn_post", KT), ("b_gate", 16), ("shift_mu", 14), ("w0", CT), ("a0", CT), ("k_k", CT),
                 ("k_a", CT), ("r_k", CT), ("lnx_w", CT), ("lnx_b", CT), ("s5_re", 16), ("s5_im", 16),
                 ("s5_step", 16), ("s5_d", CT), ("b_glu", CT), ("ffn_conv_w", 3 * 2 * FF_T),
                 ("ffn_conv_b", 2 * FF_T)]
PARAMS = Columns(PARAM_WIDTHS)


def layer_chunks(l):
    names = [("in", l, j) for j in range(6)]
    names += [("in", l, j) for j in (6, 7, 8, 9)]
    names += [("mem_kv", l, 0), ("mem_kv", l, 1)]
    for b in range(3):
        if b:
            names.append((("br_conv", "br_mem")[b - 1], l, 0))
        for half in range(2):
            names.append(("in", l, 10 + 2 * b + half))
            if b == 0:
                names.append(("br_attn", l, half))
    names += [("out", l, 0), ("out", l, 1)]
    return names


def expert_chunks(l):
    names = []
    for n in range(N_BLOCKS):
        names += [("gate", l, n), ("up", l, n)]
        if n:
            names.append(("down", l, n - 1))
    return names + [("down", l, N_BLOCKS - 1)]


SECOND = [("in2", 0, j) for j in range(6)] + [("br_rwkv", 0, 0), ("in2", 0, 6), ("in2", 0, 7), ("br_s5", 0, 0),
                                              ("in2", 0, 8), ("out2", 0, 0), ("out2", 0, 1)]
SECOND += [("ffn_up", 0, _j) for _j in range(FF_T // 2)]
SECOND += [("ffn_down", 0, _j) for _j in range(6)]
ALWAYS_USED = 2 * SEQ // P
EXPERT_PART = {"gate": 0, "up": 1, "down": 2}


def static_names():
    out = []
    for l in range(DEPTH):
        out += layer_chunks(l)
    return out + SECOND


def stream_names():
    out = []
    for l in range(DEPTH):
        out += layer_chunks(l) + expert_chunks(l)
    return out + SECOND


class Banks:

    def __init__(self, ps, full, free):
        self.ps, self.full, self.free = ps, full, free
        self.uses, self.of, self.turn = [0] * 8, {}, 0

    def plan(self, key, bank=None):
        if bank is None:
            bank, self.turn = self.turn, (self.turn + 1) % 8
        self.of[key] = (bank, self.uses[bank])
        self.uses[bank] += 1

    def bank(self, key):
        return self.ps[self.of[key][0]]

    def vacant(self, key):
        b, n = self.of[key]
        return self.free[b], n

    def full_sem(self, key):
        return self.full[self.of[key][0]]

    def made(self, key):
        b, n = self.of[key]
        return self.full[b], n + 1

    def free_sem(self, key):
        return self.free[self.of[key][0]]

    def read_done(self, key):
        b, n = self.of[key]
        return self.free[b], n + 1


class Tally:

    def __init__(self, sem):
        self.sem, self.base, self.made = sem, 0, 0

    def up(self):
        self.made += 1
        return self.sem

    def at(self, n):
        return self.sem, self.base + n

    def last(self):
        return self.sem, self.made


class Machine:
    def __init__(self, nc, ctx, dram):
        self.nc, self.ctx, self.dram = nc, ctx, dram
        sb, sem = self.sb, self.sem
        self.const = sb("const", [P, len(CONST_NAMES), P])
        self.small = sb("small", [P, 64])
        self.par = sb("par", [P, PARAMS.total])
        self.wr = sb("wr", [P, KT, E_N])
        self.XT = sb("XT", [P, KT, SEQ])
        self.memT = sb("memT", [P, KT, MEM])
        self.rotary = sb("rotary", [P, 2, SEQ])
        self.cos, self.sin = self.rotary[:, 0, :], self.rotary[:, 1, :]
        self.B = [sb(f"B{i}", [P, KT, SEQ]) for i in range(6)]
        self.tmp = sb("tmp", [P, 4, SEQ])
        self.T = [self.tmp[:, i, :] for i in range(4)]
        self.v = sb("vecs", [P, 64])
        self.v2 = sb("chunk_ends", [P, 64])
        self.rt = sb("rt", [P, SEQ])
        self.s5 = sb("s5_columns", [P, 3, 16])
        self.ring = [sb(f"ring{i}", [P, 4096]) for i in range(RING)]
        ps = [ctx.enter_context(nc.psum_tensor(f"bank{i}", [P, 512], F32)) for i in range(8)]
        self.banks = Banks(ps, [sem(f"bank_full{i}") for i in range(8)], [sem(f"bank_free{i}") for i in range(8)])
        self.ring_full = [sem(f"ring_full{i}") for i in range(RING)]
        self.tallies = {}
        self.table_inputs, self.loaded, self.stored = sem("table_inputs"), sem("loaded"), sem("stored")
        self.load_n = self.store_n = 0
        self.pool_dma, self.pool_n = sem("pool_dma"), 0
        self.stream = stream_names()
        self.index = {n: i for i, n in enumerate(self.stream)}
        self.issued = 0
        self.last_uses = {}
        self.routed = set()

    def sb(self, name, shape, dt=F32):
        return self.ctx.enter_context(self.nc.sbuf_tensor(name, shape, dt))

    def sem(self, name):
        return self.ctx.enter_context(self.nc.semaphore(name))

    def c(self, name):
        return self.const[:, CONST_NAMES.index(name), :]

    def p(self, name, i=None):
        a, b = PARAMS.at[name]
        return self.par[:, a:b] if i is None else self.par[:, a + i:a + i + 1]

    def tally(self, name):
        if name not in self.tallies:
            self.tallies[name] = Tally(self.sem(name))
        return self.tallies[name]

    def landed(self, name):
        i = self.index[name]
        return self.ring_full[i % RING], 16 * (i // RING + 1)

    def slot_of(self, name):
        return self.ring[self.index[name] % RING]

    def last_use(self, name, key):
        b, use = self.banks.of[key]
        self.last_uses[self.index[name]] = (self.banks.full[b], use + 1)

    def issue_weights(self, block):
        @block.sync
        def _(sp):
            static = {n: i for i, n in enumerate(static_names())}
            while self.issued < len(self.stream):
                i = self.issued
                name = self.stream[i]
                kind, l, n = name
                if kind in EXPERT_PART and l not in self.routed:
                    break
                if i >= RING:
                    if i - RING not in self.last_uses:
                        break
                    sp.wait_ge(*self.last_uses[i - RING])
                slot = self.ring[i % RING]
                if kind in EXPERT_PART:
                    e = sp.value_load(self.block_expert[0:1, n:n + 1], min_val=0, max_val=E_N - 1)
                    used = sp.value_load(self.block_used[0:1, n:n + 1], min_val=0, max_val=1)
                    at = e * 3 + (l * E_N * 3 + EXPERT_PART[kind])
                    src = self.dram["w_expert"][bass.ds(at, 1), :, :].rearrange("n p c -> p (n c)")
                    sp.dma_start(slot[:, :], src, cond=used, bounds_check="skip_entire_dma").then_inc(self.ring_full[i % RING], 16)
                else:
                    src = self.dram["w_static"][static[name], :, :]
                    sp.dma_start(slot[:, :], src).then_inc(self.ring_full[i % RING], 16)
                self.issued += 1

    def stage(self):
        for s in self.tallies.values():
            s.base = s.made
        return self.nc.Block()


def load_inputs(m):
    d = m.dram
    with m.stage() as block:
        @block.scalar
        def _(act):
            for dst, src in ((m.B[4][:, 0, :].bitcast(I32), d["positions"]), (m.small[:, :], d["small"]),
                             (m.B[4][:, 1, :], d["lambdas"])):
                act.dma_start(dst, src).then_inc(m.table_inputs, 16)
            for dst, src in ((m.XT[:, :, :], d["xT"]), (m.const[:, :, :], d["consts"]), (m.par[:, :], d["params"])):
                act.dma_start(dst, src).then_inc(m.loaded, 16)
                m.load_n += 16
            act.wait_ge(m.table_inputs, 3 * 16)

        @block.vector
        def _(dve):
            dve.memset(m.B[5][:, 0:2, :], 0.0)


def angle_tables(m):
    ang, k, half = m.T[0], m.T[1], m.T[2]
    with m.stage() as block:
        @block.vector
        def _(dve):
            pos = m.B[4][:, 0, :].bitcast(I32)
            dve.tensor_copy(ang[:, :], pos).then_inc(m.tally("dve_step").up(), 1)
            dve.wait_ge(*m.tally("dve_step").last())
            dve.tensor_scalar(ang[:, :], ang[:, :], m.small[:, INV_FREQ], None, ALU.mult).then_inc(m.tally("dve_step").up(), 1)
            dve.wait_ge(*m.tally("dve_step").last())
            reduce_angle(m, dve, ang, k)

        m.issue_weights(block)
    with m.stage() as block:
        @block.sync
        def _(sp):
            for dst, src in ((m.memT[:, :, :], m.dram["memT"]), (m.wr[:, :, :], m.dram["w_router"])):
                sp.dma_start(dst, src).then_inc(m.loaded, 16)
                m.load_n += 16

        @block.scalar
        def _(act):
            act.activation(m.sin[:, :], ang[:, :], ACT.Sin)
            act.activation(half[:, :], ang[:, :], ACT.Sin, scale=0.5).then_inc(m.tally("half_sine").up(), 1)

        @block.vector
        def _(dve):
            dve.wait_ge(*m.tally("half_sine").at(1))
            dve.tensor_tensor(half[:, :], half[:, :], half[:, :], ALU.mult).then_inc(m.tally("dve_step").up(), 1)
            dve.wait_ge(*m.tally("dve_step").last())
            dve.tensor_scalar(m.cos[:, :], half[:, :], -2.0, 1.0, ALU.mult, ALU.add)


def reduce_angle(m, dve, ang, k):
    dve.tensor_scalar(k[:, :], ang[:, :], 1.0 / (2.0 * math.pi), MAGIC, ALU.mult, ALU.add).then_inc(m.tally("dve_step").up(), 1)
    dve.wait_ge(*m.tally("dve_step").last())
    dve.tensor_scalar(k[:, :], k[:, :], -MAGIC, None, ALU.add).then_inc(m.tally("dve_step").up(), 1)
    dve.wait_ge(*m.tally("dve_step").last())
    for part in (TWO_PI_1, TWO_PI_2, TWO_PI_3):
        dve.scalar_tensor_tensor(ang[:, :], k[:, :], -part, ang[:, :], ALU.mult, ALU.add).then_inc(m.tally("dve_step").up(), 1)
        dve.wait_ge(*m.tally("dve_step").last())
    dve.tensor_scalar(ang[:, :], ang[:, :], 3.1415925, -3.1415925, ALU.min, ALU.max).then_inc(m.tally("dve_step").up(), 1)
    dve.wait_ge(*m.tally("dve_step").last())


def project(m, pe, key, w, col, kts=KT, rhs=None):
    rhs = rhs or (lambda k: m.XT[:, k, :])
    pe.wait_ge(*m.banks.vacant(key))
    bank = m.banks.bank(key)
    for k in range(kts):
        ins = pe.matmul(bank[:, :], w(k, col), rhs(k), start=k == 0, stop=k == kts - 1)
    ins.then_inc(m.banks.full_sem(key), 1)


def by512(slot):
    v = slot[:, :].rearrange("p (k n) -> p k n", k=8)
    return lambda k, c: v[:, k, c * P:(c + 1) * P]


def by1024(slot):
    v = slot[:, :].rearrange("p (k n) -> p k n", k=4)
    return lambda k, c: v[:, k, c * P:(c + 1) * P]


def qkv(m, l):
    bk = m.banks
    raw = [m.B[3], m.B[4]]
    out = [m.B[0], m.B[1]]
    tiles = [(w, j) for w in range(2) for j in range(KT)]
    with m.stage() as block:
        for i, (w, j) in enumerate(tiles):
            bk.plan(("qk", l, w, j))
            if i:
                bk.plan(("rot", l, *tiles[i - 1]))
        for n in range(8):
            bk.plan(("v", l, n))
            if n == 0:
                bk.plan(("rot", l, *tiles[-1]))

        @block.gpsimd
        def _(pool):
            for n in range(N_BLOCKS if l == 0 else 0):
                pool.dma_start(m.dram["slots_x"][n * P:(n + 1) * P, :], m.B[5][:, 0:2, :]).then_inc(m.pool_dma, 16)
                m.pool_n += 16

        @block.tensor
        def _(pe):
            pe.wait_ge(m.loaded, m.load_n)

            def rotate(w, j):
                pe.wait_ge(*m.tally("raw_tile").at(w * KT + j + 1))
                pe.wait_ge(*bk.vacant(("rot", l, w, j)))
                bank = bk.bank(("rot", l, w, j))
                pe.matmul(bank[:, :], m.c("rotate"), raw[w][:, j, :], start=True, stop=True).then_inc(bk.full_sem(("rot", l, w, j)), 1)

            for i, (w, j) in enumerate(tiles):
                name = ("in", l, i // 4)
                pe.wait_ge(*m.landed(name))
                slot = m.slot_of(name)
                project(m, pe, ("qk", l, w, j), by512(slot), j % 4)
                if j % 4 == 3:
                    m.last_use(name, ("qk", l, w, j))
                if i:
                    rotate(*tiles[i - 1])
            for n in range(8):
                half, t = n // 4, n % 4
                name = ("in", l, 4 + half)
                pe.wait_ge(*m.landed(name))
                slot = m.slot_of(name)[:, :].rearrange("p (k n) -> p k n", k=8)
                pe.wait_ge(*bk.vacant(("v", l, n)))
                bank = bk.bank(("v", l, n))
                for k in range(KT):
                    ins = pe.matmul(bank[:, :], m.XT[:, k, t * P:(t + 1) * P], slot[:, k, :], start=k == 0, stop=k == KT - 1)
                ins.then_inc(bk.full_sem(("v", l, n)), 1)
                if t == 3:
                    m.last_use(name, ("v", l, n))
                if n == 0:
                    rotate(*tiles[-1])

        @block.scalar
        def _(act):
            for w, j in tiles:
                act.wait_ge(*bk.made(("qk", l, w, j)))
                bank = bk.bank(("qk", l, w, j))
                act.activation(raw[w][:, j, :], bank[:, :], ACT.Copy).then_inc(m.tally("raw_tile").up(), 1)
            for n in range(8):
                half, t = n // 4, n % 4
                act.wait_ge(*bk.made(("v", l, n)))
                bank = bk.bank(("v", l, n))
                act.activation(m.B[2][:, 2 * t + half, :], bank[:, :], ACT.Copy).then_inc(bk.free_sem(("v", l, n)), 1)

        @block.vector
        def _(dve):
            for i, (w, j) in enumerate(tiles):
                dve.wait_ge(*m.tally("raw_tile").at(i + 1))
                dve.tensor_tensor(out[w][:, j, :], raw[w][:, j, :], m.cos[:, :], ALU.mult).then_inc(bk.free_sem(("qk", l, w, j)), 1)
                dve.wait_ge(*bk.made(("rot", l, w, j)))
                bank = bk.bank(("rot", l, w, j))
                tmp = m.T[i % 2]
                dve.tensor_tensor(tmp[:, :], bank[:, :], m.sin[:, :], ALU.mult).then_inc(m.tally("dve_step").up(), 1)
                dve.wait_ge(*m.tally("dve_step").last())
                dve.tensor_tensor(out[w][:, j, :], out[w][:, j, :], tmp[:, :], ALU.add).then_inc(bk.free_sem(("rot", l, w, j)), 1)
                dve.wait_ge(*bk.read_done(("rot", l, w, j)))
        m.issue_weights(block)


def lam_vectors(m):
    lb = m.B[4][:, 1, :].rearrange("p (n d) -> p n d", d=64)
    dots, exps = m.v[:, 2:6], m.v[:, 50:54]
    with m.stage() as block:
        @block.vector
        def _(dve):
            dve.tensor_tensor(m.T[0][:, 0:256].rearrange("p (n d) -> p n d", d=64), lb[:, 0:8:2, :], lb[:, 1:8:2, :], ALU.mult).then_inc(m.tally("dve_step").up(), 1)
            dve.wait_ge(*m.tally("dve_step").last())
            dve.tensor_reduce(
                dots, m.T[0][:, 0:256].rearrange("p (n d) -> p n d", d=64), AX, ALU.add).then_inc(m.tally("lambda_dots").up(), 1)
            dve.memset(m.v[:, 46:50], 1.0)
            dve.wait_ge(*m.tally("lambda_exps").at(1))
            for l in range(DEPTH):
                lam_init = 0.8 - 0.6 * math.exp(-0.3 * l)
                dve.tensor_tensor(m.v[:, 6:7], exps[:, 2 * l + 1:2 * l + 2], exps[:, 2 * l:2 * l + 1], ALU.subtract).then_inc(m.tally("dve_step").up(), 1)
                dve.wait_ge(*m.tally("dve_step").last())
                dve.tensor_scalar(m.v[:, 47 + 2 * l:48 + 2 * l], m.v[:, 6:7], -lam_init, None, ALU.add).then_inc(m.tally("dve_step").up(), 1)
                dve.wait_ge(*m.tally("dve_step").last())

        @block.scalar
        def _(act):
            act.wait_ge(*m.tally("lambda_dots").at(1))
            act.activation(exps, dots, ACT.Exp).then_inc(m.tally("lambda_exps").up(), 1)


def softmax_attention(m, l, kind, n_heads, comps, keys_of, score, values, out, scale, buf, mask):
    bk = m.banks
    units = [(h, qb) for h in range(n_heads) for qb in range(TT)]
    n_u = len(units)
    prob, mix, mixT = buf
    key = lambda what, *i: (kind + what, l, *i)
    with m.stage() as block:
        for i in range(n_u + 3):
            if i < n_u:
                for c in range(comps):
                    bk.plan(key("score", i, c), (i % 2) * 2 + c)
            if 2 <= i < n_u + 2:
                bk.plan(key("T", i - 2), 4 + i % 2)
            if i >= 3 and units[i - 3][1] == 0:
                bk.plan(key("pv", units[i - 3][0]), 6 + units[i - 3][0] % 2)

        @block.tensor
        def _(pe):
            for i in range(n_u + 3):
                if i < n_u:
                    h, qb = units[i]
                    nk = keys_of(qb)
                    for c in range(comps):
                        pe.wait_ge(*bk.vacant(key("score", i, c)))
                        bank = bk.bank(key("score", i, c))
                        q, k = score(h, qb, c)
                        ins = pe.matmul(bank[:, 0:nk], q, k, start=True, stop=not mask)
                        if mask:
                            ins = pe.matmul(bank[:, nk - P:nk], m.c("ident"), m.c("causal"), start=False, stop=True)
                        ins.then_inc(bk.full_sem(key("score", i, c)), 1)
                if 2 <= i < n_u + 2:
                    u = i - 2
                    nk = keys_of(units[u][1])
                    pe.wait_ge(*m.tally("mixed_probs").at(u + 1))
                    pe.wait_ge(*bk.vacant(key("T", u)))
                    bank = bk.bank(key("T", u))
                    for kb in range(nk // P):
                        ins = pe.transpose(bank[:, kb * P:(kb + 1) * P], mix[u % 2][:, kb * P:(kb + 1) * P], m.c("ident"))
                    ins.then_inc(bk.full_sem(key("T", u)), 1)
                if i >= 3:
                    u = i - 3
                    h, qb = units[u]
                    nk = keys_of(qb)
                    pe.wait_ge(*bk.read_done(key("T", u)))
                    if qb == 0:
                        pe.wait_ge(*bk.vacant(key("pv", h)))
                    bank = bk.bank(key("pv", h))
                    for kb in range(nk // P):
                        ins = pe.matmul(bank[:, qb * P:(qb + 1) * P], values(h, kb), mixT[u % 2][:, kb * P:(kb + 1) * P],
                                        start=kb == 0, stop=kb == nk // P - 1)
                    if qb == TT - 1:
                        ins.then_inc(bk.full_sem(key("pv", h)), 1)
                    else:
                        ins.then_inc(m.tally("partial_output").up(), 1)

        def pv_done(eng, u):
            h, qb = units[u]
            if qb == TT - 1:
                eng.wait_ge(*bk.made(key("pv", h)))
            else:
                eng.wait_ge(*m.tally("partial_output").at(h * (TT - 1) + qb + 1))

        def finish(act, h):
            act.wait_ge(*bk.made(key("pv", h)))
            bank = bk.bank(key("pv", h))
            act.activation(out[:, h, :], bank[:, :], ACT.Copy).then_inc(bk.free_sem(key("pv", h)), 1)

        v = m.v

        @block.vector
        def _(dve):
            def maxima(i):
                nk = keys_of(units[i][1])
                for c in range(comps):
                    dve.wait_ge(*bk.made(key("score", i, c)))
                    bank = bk.bank(key("score", i, c))
                    ins = dve.tensor_reduce(v[:, 8 + (i % 2) * 2 + c:9 + (i % 2) * 2 + c], bank[:, 0:nk], AX, ALU.max)
                ins.then_inc(m.tally("dve_step").up(), 1)
                dve.wait_ge(*m.tally("dve_step").last())
                dve.tensor_scalar(
                    v[:, 12 + (i % 2) * 2:12 + (i % 2) * 2 + comps], v[:, 8 + (i % 2) * 2:8 + (i % 2) * 2 + comps],
                    -scale, None, ALU.mult).then_inc(m.tally("scaled_maxima").up(), 1)

            maxima(0)
            for i in range(n_u):
                if i + 1 < n_u:
                    maxima(i + 1)
                h, qb = units[i]
                nk = keys_of(qb)
                s = (i % 2) * 2
                dve.wait_ge(*m.tally("probs").at(i + 1))
                if i >= 2:
                    dve.wait_ge(*bk.made(key("T", i - 2)))
                dve.reciprocal(v[:, 20 + s:20 + s + comps], v[:, 16 + s:16 + s + comps]).then_inc(m.tally("dve_step").up(), 1)
                dve.wait_ge(*m.tally("dve_step").last())
                if comps == 2:
                    dve.tensor_tensor(v[:, 24:26], v[:, 20 + s:22 + s], v[:, 46 + 2 * l:48 + 2 * l], ALU.mult).then_inc(m.tally("dve_step").up(), 1)
                    dve.wait_ge(*m.tally("dve_step").last())
                    dve.tensor_scalar(m.T[0][:, 0:nk], prob[i % 2][1][:, 0:nk], v[:, 25:26], None, ALU.mult).then_inc(m.tally("dve_step").up(), 1)
                    dve.wait_ge(*m.tally("dve_step").last())
                    ins = dve.scalar_tensor_tensor(mix[i % 2][:, 0:nk], prob[i % 2][0][:, 0:nk], v[:, 24:25],
                                                   m.T[0][:, 0:nk], ALU.mult, ALU.add)
                else:
                    ins = dve.tensor_scalar(mix[i % 2][:, 0:nk], prob[i % 2][0][:, 0:nk], v[:, 20 + s:21 + s], None, ALU.mult)
                ins.then_inc(m.tally("mixed_probs").up(), 1)
                dve.wait_ge(*m.tally("mixed_probs").at(i + 1))

        @block.scalar
        def _(act):
            for i in range(n_u + 2):
                if i < n_u:
                    nk = keys_of(units[i][1])
                    s = (i % 2) * 2
                    act.wait_ge(*m.tally("scaled_maxima").at(i + 1))
                    if i >= 2:
                        act.wait_ge(*m.tally("mixed_probs").at(i - 1))
                    for c in range(comps):
                        act.wait_ge(*bk.made(key("score", i, c)))
                        bank = bk.bank(key("score", i, c))
                        ins = act.activation(prob[i % 2][c][:, 0:nk], bank[:, 0:nk], ACT.Exp,
                                             bias=v[:, 12 + s + c:13 + s + c], scale=scale,
                                             accum_out=v[:, 16 + s + c:17 + s + c])
                        ins.then_inc(bk.free_sem(key("score", i, c)), 1)
                    for c in range(comps):
                        act.wait_ge(*bk.read_done(key("score", i, c)))
                    act.activation(v[:, 30:31], v[:, 16 + s:17 + s], ACT.Copy).then_inc(m.tally("probs").up(), 1)
                if i >= 2:
                    u = i - 2
                    h, qb = units[u]
                    nk = keys_of(qb)
                    act.wait_ge(*bk.made(key("T", u)))
                    bank = bk.bank(key("T", u))
                    if u >= 2:
                        pv_done(act, u - 2)
                    act.activation(mixT[u % 2][:, 0:nk], bank[:, 0:nk], ACT.Copy).then_inc(bk.free_sem(key("T", u)), 1)
                    if u >= 1 and units[u - 1][1] == TT - 1:
                        finish(act, units[u - 1][0])
            finish(act, n_heads - 1)

        m.issue_weights(block)


def attention(m, l):
    q, k, v = m.B[0], m.B[1], m.B[2]
    tmp = m.B[4]
    buf = ([[tmp[:, 2 * i + c, :] for c in range(2)] for i in range(2)], [tmp[:, 4, :], tmp[:, 5, :]],
           [tmp[:, 6, :], tmp[:, 7, :]])

    def score(h, qb, c):
        rows = slice(64 * c, 64 * c + 64)
        return q[rows, h, qb * P:(qb + 1) * P], k[rows, h, 0:(qb + 1) * P]

    def values(h, kb):
        return v[:, 2 * kb + h // 4, (h % 4) * P:(h % 4 + 1) * P]

    softmax_attention(m, l, "att", HEADS, 2, lambda qb: (qb + 1) * P, score, values, m.B[3], 64 ** -0.5, buf, True)


def conv_and_memory_inputs(m, l):
    bk = m.banks
    att, sq = m.B[3], m.B[4]
    lam_init = 0.8 - 0.6 * math.exp(-0.3 * l)
    cb, cc, cu, z = m.B[0], m.B[0], m.B[1], m.B[1]
    dest = [m.B[0][:, j, :] for j in range(8)] + [m.B[1][:, j, :] for j in range(4)] + [m.B[5][:, j, :] for j in range(4)]
    kmT = m.B[5][:, 4:6, :].rearrange("p a (b t) -> p (a b) t", b=2)
    with m.stage() as block:
        for j in range(16):
            bk.plan(("cm", l, j))
            if j < HEADS:
                bk.plan(("rms", l, j))
        for j in range(6):
            bk.plan(("mk", l, j))

        @block.tensor
        def _(pe):
            for j in range(16):
                name = ("in", l, 6 + j // 4)
                pe.wait_ge(*m.landed(name))
                slot = m.slot_of(name)
                project(m, pe, ("cm", l, j), by512(slot), j % 4)
                if j % 4 == 3:
                    m.last_use(name, ("cm", l, j))
                if j < HEADS:
                    pe.wait_ge(*m.tally("squares").at(j + 1))
                    pe.wait_ge(*bk.vacant(("rms", l, j)))
                    bank = bk.bank(("rms", l, j))
                    pe.matmul(bank[:, :], m.c("ones"), sq[:, j, :], start=True, stop=True).then_inc(bk.full_sem(("rms", l, j)), 1)
            pe.wait_ge(*m.landed(("mem_kv", l, 0)))
            slot = by512(m.slot_of(("mem_kv", l, 0)))
            for j in range(4):
                pe.wait_ge(*bk.vacant(("mk", l, j)))
                bank = bk.bank(("mk", l, j))
                for k in range(KT):
                    ins = pe.matmul(bank[:, 0:MEM], slot(k, j), m.memT[:, k, :], start=k == 0, stop=k == KT - 1)
                ins.then_inc(bk.full_sem(("mk", l, j)), 1)
            m.last_use(("mem_kv", l, 0), ("mk", l, 3))
            pe.wait_ge(*m.landed(("mem_kv", l, 1)))
            slot = m.slot_of(("mem_kv", l, 1))[:, :].rearrange("p (k n) -> p k n", k=8)
            for j in range(2):
                pe.wait_ge(*bk.vacant(("mk", l, 4 + j)))
                bank = bk.bank(("mk", l, 4 + j))
                for k in range(KT):
                    ins = pe.matmul(bank[:, :], m.memT[:, k, j * P:(j + 1) * P], slot[:, k, :], start=k == 0, stop=k == KT - 1)
                ins.then_inc(bk.full_sem(("mk", l, 4 + j)), 1)
            m.last_use(("mem_kv", l, 1), ("mk", l, 5))

        @block.scalar
        def _(act):
            act.activation(sq[:, 0, :], att[:, 0, :], ACT.Square).then_inc(m.tally("squares").up(), 1)
            for j in range(16):
                if j + 1 < HEADS:
                    act.activation(sq[:, j + 1, :], att[:, j + 1, :], ACT.Square).then_inc(m.tally("squares").up(), 1)
                act.wait_ge(*bk.made(("cm", l, j)))
                bank = bk.bank(("cm", l, j))
                act.activation(dest[j], bank[:, :], ACT.Copy).then_inc(bk.free_sem(("cm", l, j)), 1)
                if j == HEADS:
                    for h in range(HEADS):
                        act.wait_ge(*m.tally("mean_squares").at(h + 1))
                        act.activation(sq[:, h, :], sq[:, h, :], ACT.Sqrt).then_inc(m.tally("roots").up(), 1)
            for j in range(4):
                act.wait_ge(*bk.made(("mk", l, j)))
                bank = bk.bank(("mk", l, j))
                act.activation(kmT[:, j, :], bank[:, 0:MEM], ACT.Copy).then_inc(bk.free_sem(("mk", l, j)), 1)
            for j in range(2):
                act.wait_ge(*bk.made(("mk", l, 4 + j)))
                bank = bk.bank(("mk", l, 4 + j))
                act.activation(m.B[5][:, 6 + j, :], bank[:, :], ACT.Copy).then_inc(bk.free_sem(("mk", l, 4 + j)), 1)

        @block.vector
        def _(dve):
            dve.tensor_scalar(m.v[:, 32:33], m.p(f"subln{l}"), 1.0 - lam_init, None, ALU.mult).then_inc(m.tally("dve_step").up(), 1)
            dve.wait_ge(*m.tally("dve_step").last())
            for h in range(HEADS):
                dve.wait_ge(*bk.made(("rms", l, h)))
                bank = bk.bank(("rms", l, h))
                dve.tensor_scalar(sq[:, h, :], bank[:, :], 1.0 / P, RMS_EPS, ALU.mult, ALU.add).then_inc(bk.free_sem(("rms", l, h)), 1)
                dve.wait_ge(*bk.read_done(("rms", l, h)))
                dve.tensor_scalar(att[:, h, :], att[:, h, :], m.v[:, 32:33], None, ALU.mult).then_inc(m.tally("mean_squares").up(), 1)
            for h in range(HEADS):
                dve.wait_ge(*m.tally("roots").at(h + 1))
                dve.reciprocal(sq[:, h, :], sq[:, h, :]).then_inc(m.tally("dve_step").up(), 1)
                dve.wait_ge(*m.tally("dve_step").last())
                dve.tensor_tensor(att[:, h, :], att[:, h, :], sq[:, h, :], ALU.mult).then_inc(m.tally("dve_step").up(), 1)
                dve.wait_ge(*m.tally("dve_step").last())
            dve.wait_ge(*bk.read_done(("cm", l, 11)))
            for j in range(CT):
                w = lambda tap: m.p(f"conv_w{l}", tap * CT + j)
                zt, y = m.B[1][:, 4 + j, :], m.B[2][:, j, :]
                dve.tensor_tensor(zt, m.B[0][:, 4 + j, :], m.B[1][:, j, :], ALU.mult).then_inc(m.tally("dve_step").up(), 1)
                dve.wait_ge(*m.tally("dve_step").last())
                dve.tensor_scalar(y, zt, w(2), None, ALU.mult).then_inc(m.tally("dve_step").up(), 1)
                dve.wait_ge(*m.tally("dve_step").last())
                dve.scalar_tensor_tensor(y[:, 1:SEQ], zt[:, 0:SEQ - 1], w(1), y[:, 1:SEQ], ALU.mult, ALU.add).then_inc(m.tally("dve_step").up(), 1)
                dve.wait_ge(*m.tally("dve_step").last())
                dve.scalar_tensor_tensor(y[:, 2:SEQ], zt[:, 0:SEQ - 2], w(0), y[:, 2:SEQ], ALU.mult, ALU.add).then_inc(m.tally("dve_step").up(), 1)
                dve.wait_ge(*m.tally("dve_step").last())
                dve.tensor_tensor(y, y, m.B[0][:, j, :], ALU.mult).then_inc(m.tally("dve_step").up(), 1)
                dve.wait_ge(*m.tally("dve_step").last())
        m.issue_weights(block)


def memory_attention(m, l):
    tmp = m.B[4]
    kmT = m.B[5][:, 4:6, :].rearrange("p a (b t) -> p (a b) t", b=2)
    buf = ([[tmp[:, 2 * i + c, :] for c in range(2)] for i in range(2)], [tmp[:, 4, :], tmp[:, 5, :]],
           [tmp[:, 6, :], tmp[:, 7, :]])
    softmax_attention(m, l, "mem", MEM_HEADS, 1, lambda qb: MEM,
                      lambda h, qb, c: (m.B[5][:, h, qb * P:(qb + 1) * P], kmT[:, h, :]),
                      lambda h, kb: m.B[5][:, 6 + kb, h * P:(h + 1) * P],
                      m.B[2][:, 4:8, :], P ** -0.5, buf, False)


def merge(m, l):
    bk = m.banks
    merged, sig = m.B[0], m.B[1]
    rhs = [lambda k: m.B[3][:, k, :], lambda k: m.B[2][:, k, :], lambda k: m.B[2][:, 4 + k, :]]
    jobs = [(b, j) for b in range(3) for j in range(KT)]
    with m.stage() as block:
        for b, j in jobs:
            bk.plan(("gate", l, b, j))
            bk.plan(("branch", l, b, j))

        @block.tensor
        def _(pe):
            for b, j in jobs:
                g = ("in", l, 10 + 2 * b + j // 4)
                pe.wait_ge(*m.landed(g))
                project(m, pe, ("gate", l, b, j), by512(m.slot_of(g)), j % 4)
                if j % 4 == 3:
                    m.last_use(g, ("gate", l, b, j))
                if b == 0:
                    w = ("br_attn", l, j // 4)
                    pe.wait_ge(*m.landed(w))
                    project(m, pe, ("branch", l, b, j), by512(m.slot_of(w)), j % 4, KT, rhs[0])
                    if j % 4 == 3:
                        m.last_use(w, ("branch", l, b, j))
                else:
                    w = (("br_conv", "br_mem")[b - 1], l, 0)
                    pe.wait_ge(*m.landed(w))
                    project(m, pe, ("branch", l, b, j), by1024(m.slot_of(w)), j, CT, rhs[b])
                    if j == KT - 1:
                        m.last_use(w, ("branch", l, b, j))

        @block.scalar
        def _(act):
            for i, (b, j) in enumerate(jobs):
                act.wait_ge(*bk.made(("gate", l, b, j)))
                bank = bk.bank(("gate", l, b, j))
                if i >= 4:
                    act.wait_ge(*bk.read_done(("branch", l, *jobs[i - 4])))
                act.activation(sig[:, i % 4, :], bank[:, :], ACT.Sigmoid).then_inc(bk.free_sem(("gate", l, b, j)), 1)

        @block.vector
        def _(dve):
            for i, (b, j) in enumerate(jobs):
                dve.wait_ge(*bk.read_done(("gate", l, b, j)))
                dve.wait_ge(*bk.made(("branch", l, b, j)))
                bank = bk.bank(("branch", l, b, j))
                if b == 0:
                    dve.tensor_tensor(merged[:, j, :], bank[:, :], sig[:, i % 4, :], ALU.mult).then_inc(bk.free_sem(("branch", l, b, j)), 1)
                    continue
                t = sig[:, 4 + i % 4, :]
                dve.tensor_tensor(t, bank[:, :], sig[:, i % 4, :], ALU.mult).then_inc(bk.free_sem(("branch", l, b, j)), 1)
                dve.wait_ge(*bk.read_done(("branch", l, b, j)))
                dve.tensor_tensor(merged[:, j, :], merged[:, j, :], t, ALU.add).then_inc(m.tally("dve_step").up(), 1)
                dve.wait_ge(*m.tally("dve_step").last())
        m.issue_weights(block)


def out_projection(m, l):
    bk = m.banks
    with m.stage() as block:
        for j in range(KT):
            bk.plan(("mix", l, j))

        @block.tensor
        def _(pe):
            for j in range(KT):
                name = ("out", l, j // 4)
                pe.wait_ge(*m.landed(name))
                project(m, pe, ("mix", l, j), by512(m.slot_of(name)), j % 4, KT, lambda k: m.B[0][:, k, :])
                if j % 4 == 3:
                    m.last_use(name, ("mix", l, j))

        @block.vector
        def _(dve):
            for j in range(KT):
                dve.wait_ge(*bk.made(("mix", l, j)))
                bank = bk.bank(("mix", l, j))
                dve.scalar_tensor_tensor(m.B[1][:, j, :], m.XT[:, j, :], ALPHA, bank[:, :], ALU.mult, ALU.add).then_inc(bk.free_sem(("mix", l, j)), 1)
        m.issue_weights(block)


def layer_norm(m, l, which):
    bk = m.banks
    t, sq = m.B[1], m.B[4]
    g, b = f"ln{which}_g{l}", f"ln{which}_b{l}"
    with m.stage() as block:
        bk.plan(("mean", l, which))
        bk.plan(("var", l, which))

        @block.tensor
        def _(pe):
            pe.wait_ge(*bk.vacant(("mean", l, which)))
            bank = bk.bank(("mean", l, which))
            for k in range(KT):
                ins = pe.matmul(bank[:, :], m.c("ones_over_d"), t[:, k, :], start=k == 0, stop=k == KT - 1)
            ins.then_inc(bk.full_sem(("mean", l, which)), 1)
            pe.wait_ge(*bk.vacant(("var", l, which)))
            bank = bk.bank(("var", l, which))
            for k in range(KT):
                pe.wait_ge(*m.tally("squares").at(k + 1))
                ins = pe.matmul(bank[:, :], m.c("ones_over_d"), sq[:, k, :], start=k == 0, stop=k == KT - 1)
            ins.then_inc(bk.full_sem(("var", l, which)), 1)

        @block.vector
        def _(dve):
            dve.wait_ge(*bk.made(("mean", l, which)))
            bank = bk.bank(("mean", l, which))
            for k in range(KT):
                ins = dve.tensor_tensor(t[:, k, :], t[:, k, :], bank[:, :], ALU.subtract)
                ins.then_inc(m.tally("deviations").up(), 1)
            dve.wait_ge(*m.tally("deviations").at(KT))
            dve.memset(m.v[:, 40:41], 0.0).then_inc(bk.free_sem(("mean", l, which)), 1)
            dve.wait_ge(*bk.made(("var", l, which)))
            bank = bk.bank(("var", l, which))
            dve.tensor_scalar(m.T[0][:, :], bank[:, :], LN_EPS, None, ALU.add).then_inc(bk.free_sem(("var", l, which)), 1)
            dve.wait_ge(*m.tally("roots").at(1))
            dve.reciprocal(m.T[1][:, :], m.T[0][:, :]).then_inc(m.tally("dve_step").up(), 1)
            dve.wait_ge(*m.tally("dve_step").last())
            for k in range(KT):
                dve.tensor_tensor(t[:, k, :], t[:, k, :], m.T[1][:, :], ALU.mult).then_inc(m.tally("normalised").up(), 1)

        @block.scalar
        def _(act):
            for k in range(KT):
                act.wait_ge(*m.tally("deviations").at(k + 1))
                act.activation(sq[:, k, :], t[:, k, :], ACT.Square).then_inc(m.tally("squares").up(), 1)
            act.wait_ge(*bk.read_done(("var", l, which)))
            act.activation(m.T[0][:, :], m.T[0][:, :], ACT.Sqrt).then_inc(m.tally("roots").up(), 1)
            for k in range(KT):
                act.wait_ge(*m.tally("normalised").at(k + 1))
                act.activation(m.XT[:, k, :], t[:, k, :], ACT.Identity, bias=m.p(b, k), scale=m.p(g, k))
        m.issue_weights(block)


def route(m, l):
    bk = m.banks
    R = m.B[5]
    at = [0]

    def area(*shape):
        n = int(np.prod(shape))
        a = R[:, :, :].rearrange("p a b -> p (a b)")[:, at[0]:at[0] + n]
        at[0] += n
        if len(shape) == 2:
            a = a.rearrange("p (a b) -> p a b", a=shape[0])
        if len(shape) == 3:
            a = a.rearrange("p (a b c) -> p a b c", a=shape[0], b=shape[1])
        return a
    logit, score, masked, tmp = area(TT, E_N), area(TT, E_N), area(TT, E_N), area(TT, E_N)
    first, second, both, rank = area(TT, E_N), area(TT, E_N), area(TT, E_N), area(TT, E_N)
    gmax, gsel, gtmp = area(TT, G_N), area(TT, G_N), area(TT, G_N)
    m1, m2, s1 = area(TT), area(TT), area(TT)
    cnt, padded, pend, pstart = area(E_N), area(E_N), area(E_N), area(E_N)
    cmp = area(N_BLOCKS, E_N)
    nblk = area(N_BLOCKS)
    slotf = area(2, TT)
    xtok = m.B[0][:, :, :].rearrange("p (t a) b -> p t (a b)", t=TT)
    bc = lambda a: a.unsqueeze(2).broadcast_to([P, TT, E_N])
    ekey = m.small[:, EXPERT_KEY].unsqueeze(1).broadcast_to([P, TT, E_N])
    gkey = m.small[:, GROUP_KEY].unsqueeze(1).broadcast_to([P, TT, G_N])

    with m.stage() as block:
        bk.plan(("logit", l))
        for i in range(8):
            bk.plan(("xtok", l, i))

        @block.tensor
        def _(pe):
            pe.wait_ge(*bk.vacant(("logit", l)))
            bank = bk.bank(("logit", l))
            for t in range(TT):
                for k in range(KT):
                    ins = pe.matmul(bank[:, t * E_N:(t + 1) * E_N], m.XT[:, k, t * P:(t + 1) * P], m.wr[:, k, :],
                                    start=k == 0, stop=k == KT - 1)
            ins.then_inc(bk.full_sem(("logit", l)), 1)
            for i in range(8):
                t, half = i // 2, i % 2
                pe.wait_ge(*bk.vacant(("xtok", l, i)))
                bank = bk.bank(("xtok", l, i))
                for k in range(4):
                    ins = pe.transpose(bank[:, k * P:(k + 1) * P], m.XT[:, half * 4 + k, t * P:(t + 1) * P], m.c("ident"))
                ins.then_inc(bk.full_sem(("xtok", l, i)), 1)

        @block.scalar
        def _(act):
            for i in range(8):
                t, half = i // 2, i % 2
                act.wait_ge(*bk.made(("xtok", l, i)))
                bank = bk.bank(("xtok", l, i))
                act.activation(xtok[:, t, half * 512:(half + 1) * 512], bank[:, :], ACT.Copy).then_inc(bk.free_sem(("xtok", l, i)), 1)
            act.wait_ge(*m.tally("shifted_logits").at(1))
            act.activation(score, logit, ACT.Exp).then_inc(m.tally("probs").up(), 1)

        @block.vector
        def _(dve):
            dve.wait_ge(*bk.made(("logit", l)))
            bank = bk.bank(("logit", l))
            dve.tensor_tensor(logit, bank[:, 0:TT * E_N].rearrange("p (t e) -> p t e", t=TT),
                                       m.p("router_bias").unsqueeze(1).broadcast_to([P, TT, E_N]), ALU.add).then_inc(bk.free_sem(("logit", l)), 1)
            dve.wait_ge(*bk.read_done(("logit", l)))
            dve.tensor_reduce(m1, logit, AX, ALU.max).then_inc(m.tally("dve_step").up(), 1)
            dve.wait_ge(*m.tally("dve_step").last())
            dve.tensor_tensor(logit, logit, bc(m1), ALU.subtract).then_inc(m.tally("shifted_logits").up(), 1)
            dve.wait_ge(*m.tally("probs").at(1))
            dve.tensor_reduce(s1, score, AX, ALU.add).then_inc(m.tally("dve_step").up(), 1)
            dve.wait_ge(*m.tally("dve_step").last())
            dve.reciprocal(s1, s1).then_inc(m.tally("dve_step").up(), 1)
            dve.wait_ge(*m.tally("dve_step").last())
            dve.tensor_tensor(score, score, bc(s1), ALU.mult).then_inc(m.tally("dve_step").up(), 1)
            dve.wait_ge(*m.tally("dve_step").last())
            dve.tensor_reduce(gmax, score.rearrange("p t (g e) -> p t g e", g=G_N), AX, ALU.max).then_inc(m.tally("dve_step").up(), 1)
            dve.wait_ge(*m.tally("dve_step").last())
            dve.tensor_reduce(m1, gmax, AX, ALU.max).then_inc(m.tally("dve_step").up(), 1)
            dve.wait_ge(*m.tally("dve_step").last())
            dve.tensor_tensor(gtmp, gmax, m1.unsqueeze(2).broadcast_to([P, TT, G_N]), ALU.is_equal).then_inc(m.tally("dve_step").up(), 1)
            dve.wait_ge(*m.tally("dve_step").last())
            dve.tensor_tensor(gtmp, gtmp, gkey, ALU.mult).then_inc(m.tally("dve_step").up(), 1)
            dve.wait_ge(*m.tally("dve_step").last())
            dve.tensor_reduce(m1, gtmp, AX, ALU.max).then_inc(m.tally("dve_step").up(), 1)
            dve.wait_ge(*m.tally("dve_step").last())
            dve.tensor_tensor(gsel, gtmp, m1.unsqueeze(2).broadcast_to([P, TT, G_N]), ALU.is_equal).then_inc(m.tally("dve_step").up(), 1)
            dve.wait_ge(*m.tally("dve_step").last())
            g4 = gsel.unsqueeze(3).broadcast_to([P, TT, G_N, 4])
            v4 = lambda a: a.rearrange("p t (g e) -> p t g e", g=G_N)
            dve.tensor_tensor(v4(masked), v4(score), g4, ALU.mult).then_inc(m.tally("dve_step").up(), 1)
            dve.wait_ge(*m.tally("dve_step").last())
            dve.tensor_scalar(gtmp, gsel, -1.0, None, ALU.add).then_inc(m.tally("dve_step").up(), 1)
            dve.wait_ge(*m.tally("dve_step").last())
            dve.tensor_tensor(v4(masked), v4(masked), gtmp.unsqueeze(3).broadcast_to([P, TT, G_N, 4]), ALU.add).then_inc(m.tally("dve_step").up(), 1)
            dve.wait_ge(*m.tally("dve_step").last())
            for best, top in ((first, m1), (second, m2)):
                dve.tensor_reduce(top, masked, AX, ALU.max).then_inc(m.tally("dve_step").up(), 1)
                dve.wait_ge(*m.tally("dve_step").last())
                dve.tensor_tensor(tmp, masked, bc(top), ALU.is_equal).then_inc(m.tally("dve_step").up(), 1)
                dve.wait_ge(*m.tally("dve_step").last())
                dve.tensor_tensor(tmp, tmp, ekey, ALU.mult).then_inc(m.tally("dve_step").up(), 1)
                dve.wait_ge(*m.tally("dve_step").last())
                dve.tensor_reduce(s1, tmp, AX, ALU.max).then_inc(m.tally("dve_step").up(), 1)
                dve.wait_ge(*m.tally("dve_step").last())
                dve.tensor_tensor(best, tmp, bc(s1), ALU.is_equal).then_inc(m.tally("dve_step").up(), 1)
                dve.wait_ge(*m.tally("dve_step").last())
                dve.tensor_scalar(tmp, best, -4.0, None, ALU.mult).then_inc(m.tally("dve_step").up(), 1)
                dve.wait_ge(*m.tally("dve_step").last())
                dve.tensor_tensor(masked, masked, tmp, ALU.add).then_inc(m.tally("dve_step").up(), 1)
                dve.wait_ge(*m.tally("dve_step").last())
            dve.tensor_tensor(s1, m1, m2, ALU.add).then_inc(m.tally("dve_step").up(), 1)
            dve.wait_ge(*m.tally("dve_step").last())
            dve.reciprocal(s1, s1).then_inc(m.tally("dve_step").up(), 1)
            dve.wait_ge(*m.tally("dve_step").last())
            dve.tensor_tensor(m.weight[:, 0, :], m1, s1, ALU.mult).then_inc(m.tally("dve_step").up(), 1)
            dve.wait_ge(*m.tally("dve_step").last())
            dve.tensor_tensor(m.weight[:, 1, :], m2, s1, ALU.mult).then_inc(m.tally("dve_step").up(), 1)
            dve.wait_ge(*m.tally("dve_step").last())
            dve.tensor_tensor(both, first, second, ALU.add)

    with m.stage() as block:
        bk.plan(("rank", l))
        bk.plan(("count", l))

        @block.tensor
        def _(pe):
            pe.wait_ge(*bk.vacant(("rank", l)))
            bank = bk.bank(("rank", l))
            for t in range(TT):
                for u in range(t + 1):
                    ins = pe.matmul(bank[:, t * E_N:(t + 1) * E_N], m.c("ones") if u < t else m.c("earlier"),
                                    both[:, u, :], start=u == 0, stop=u == t)
            ins.then_inc(bk.full_sem(("rank", l)), 1)
            pe.wait_ge(*bk.vacant(("count", l)))
            bank = bk.bank(("count", l))
            for u in range(TT):
                ins = pe.matmul(bank[:, 0:E_N], m.c("ones"), both[:, u, :], start=u == 0, stop=u == TT - 1)
            ins.then_inc(bk.full_sem(("count", l)), 1)

        @block.vector
        def _(dve):
            dve.wait_ge(*bk.made(("rank", l)))
            bank = bk.bank(("rank", l))
            dve.tensor_copy(rank, bank[:, 0:TT * E_N].rearrange("p (t e) -> p t e", t=TT)).then_inc(bk.free_sem(("rank", l)), 1)
            dve.wait_ge(*bk.read_done(("rank", l)))
            dve.wait_ge(*bk.made(("count", l)))
            bank = bk.bank(("count", l))
            dve.tensor_scalar(cnt, bank[:, 0:E_N], 63.5, 1.0 / P, ALU.add, ALU.mult).then_inc(bk.free_sem(("count", l)), 1)
            dve.wait_ge(*bk.read_done(("count", l)))
            dve.tensor_scalar(cnt, cnt, MAGIC, None, ALU.add).then_inc(m.tally("dve_step").up(), 1)
            dve.wait_ge(*m.tally("dve_step").last())
            dve.tensor_scalar(padded, cnt, -MAGIC, float(P), ALU.add, ALU.mult).then_inc(m.tally("dve_step").up(), 1)
            dve.wait_ge(*m.tally("dve_step").last())
            dve.memset(cnt, 1.0).then_inc(m.tally("dve_step").up(), 1)
            dve.wait_ge(*m.tally("dve_step").last())
            dve.tensor_tensor_scan(pend, cnt, padded, 0.0, ALU.mult, ALU.add).then_inc(m.tally("dve_step").up(), 1)
            dve.wait_ge(*m.tally("dve_step").last())
            dve.tensor_tensor(pstart, pend, padded, ALU.subtract).then_inc(m.tally("dve_step").up(), 1)
            dve.wait_ge(*m.tally("dve_step").last())
            dve.tensor_tensor(rank, rank, pstart.unsqueeze(1).broadcast_to([P, TT, E_N]), ALU.add).then_inc(m.tally("dve_step").up(), 1)
            dve.wait_ge(*m.tally("dve_step").last())
            for i, best in enumerate((first, second)):
                dve.tensor_tensor(tmp, best, rank, ALU.mult).then_inc(m.tally("dve_step").up(), 1)
                dve.wait_ge(*m.tally("dve_step").last())
                dve.tensor_reduce(slotf[:, i, :], tmp, AX, ALU.add).then_inc(m.tally("dve_step").up(), 1)
                dve.wait_ge(*m.tally("dve_step").last())
            dve.tensor_copy(m.slot[:, :, :], slotf).then_inc(m.tally("dve_step").up(), 1)
            dve.wait_ge(*m.tally("dve_step").last())
            dve.tensor_tensor(cmp, pend.unsqueeze(1).broadcast_to([P, N_BLOCKS, E_N]),
                                 m.small[:, BLOCK_START].unsqueeze(2).broadcast_to([P, N_BLOCKS, E_N]), ALU.is_le).then_inc(m.tally("dve_step").up(), 1)
            dve.wait_ge(*m.tally("dve_step").last())
            dve.tensor_reduce(nblk, cmp, AX, ALU.add).then_inc(m.tally("dve_step").up(), 1)
            dve.wait_ge(*m.tally("dve_step").last())
            dve.tensor_scalar(m.block_expert[:, :], nblk, float(E_N - 1), None, ALU.min)
            dve.tensor_scalar(m.block_used[:, :], nblk, float(E_N) - 0.5, None, ALU.is_lt)

    with m.stage() as block:
        @block.gpsimd
        def _(pool):
            pool.wait_ge(m.pool_dma, m.pool_n)
            for i in range(2):
                for t in range(TT):
                    pool.indirect_dma_start(m.dram["slots_x"], bass.IndirectOffsetOnAxis(ap=m.slot[:, i, t:t + 1], axis=0),
                                            xtok[:, t, :], None).then_inc(m.pool_dma, 16)
                    m.pool_n += 16
            pool.wait_ge(m.pool_dma, m.pool_n)
        m.routed.add(l)
        m.issue_weights(block)


def experts(m, l):
    bk = m.banks
    xb = [m.B[1][:, 2 * i:2 * i + 2, :].rearrange("p a b -> p (a b)") for i in range(2)]
    xbT = [m.B[1][:, 4 + 2 * i:6 + 2 * i, :].rearrange("p a (b c) -> p (a b) c", c=P) for i in range(2)]
    silu = [m.B[2][:, i, :] for i in range(2)]
    hid = [m.B[2][:, 2 + i, :] for i in range(2)]
    hidT = [m.B[2][:, 4 + i, :].rearrange("p (a b) -> p a b", a=4) for i in range(2)]
    y = [m.B[3][:, 2 * i:2 * i + 2, :] for i in range(2)]
    nb = N_BLOCKS
    x_in, y_out = m.x_in, m.y_out
    with m.stage() as block:
        for n in range(nb + 1):
            if n < nb:
                for i in range(2):
                    bk.plan(("xbT", l, n, i), i)
                bk.plan(("g", l, n), 2)
                bk.plan(("u", l, n), 3)
            if n >= 1:
                bk.plan(("hT", l, n - 1), 4)
                for i in range(2):
                    bk.plan(("y", l, n - 1, i), 5 + i)

        @block.tensor
        def _(pe):
            for n in range(nb + 1):
                if n < nb:
                    pe.wait_ge(*x_in.at(n))
                    for i in range(2):
                        pe.wait_ge(*bk.vacant(("xbT", l, n, i)))
                        bank = bk.bank(("xbT", l, n, i))
                        for k in range(4):
                            c = (4 * i + k) * P
                            ins = pe.transpose(bank[:, k * P:(k + 1) * P], xb[n % 2][:, c:c + P], m.c("ident"))
                        ins.then_inc(bk.full_sem(("xbT", l, n, i)), 1)
                if n >= 1:
                    o = n - 1
                    used_before = used
                    pe.wait_ge(*m.tally("hidden_values").at(o + 1))
                    pe.wait_ge(*bk.vacant(("hT", l, o)))
                    bank = bk.bank(("hT", l, o))
                    for k in range(4):
                        ins = pe.transpose(bank[:, k * P:(k + 1) * P], hid[o % 2][:, k * P:(k + 1) * P], m.c("ident"))
                    ins.then_inc(bk.full_sem(("hT", l, o)), 1)
                if n < nb:
                    for i in range(2):
                        pe.wait_ge(*bk.read_done(("xbT", l, n, i)))
                    used = pe.value_load(m.block_used[0:1, n:n + 1], min_val=0, max_val=1) if n >= ALWAYS_USED else None
                    for what, kind in (("g", "gate"), ("u", "up")):
                        pe.wait_ge(*m.landed((kind, l, n)))
                        slot = m.slot_of((kind, l, n))[:, :].rearrange("p (k f) -> p k f", k=8)
                        pe.wait_ge(*bk.vacant((what, l, n)))
                        bank = bk.bank((what, l, n))
                        pe.matmul(bank[:, :], xbT[n % 2][:, 0, :], slot[:, 0, :], start=True, stop=False)
                        with if_used(pe, n, used):
                            for k in range(1, KT - 1):
                                pe.matmul(bank[:, :], xbT[n % 2][:, k, :], slot[:, k, :], start=False, stop=False)
                        ins = pe.matmul(bank[:, :], xbT[n % 2][:, KT - 1, :], slot[:, KT - 1, :], start=False, stop=True)
                        ins.then_inc(bk.full_sem((what, l, n)), 1)
                        m.last_use((kind, l, n), (what, l, n))
                if n >= 1:
                    o = n - 1
                    pe.wait_ge(*m.landed(("down", l, o)))
                    slot = m.slot_of(("down", l, o))[:, :].rearrange("p (k c) -> p k c", k=4)
                    pe.wait_ge(*bk.read_done(("hT", l, o)))
                    for i in range(2):
                        pe.wait_ge(*bk.vacant(("y", l, o, i)))
                        bank = bk.bank(("y", l, o, i))
                        cols = slice(i * 512, (i + 1) * 512)
                        pe.matmul(bank[:, :], hidT[o % 2][:, 0, :], slot[:, 0, cols], start=True, stop=False)
                        with if_used(pe, o, used_before):
                            for k in range(1, 3):
                                pe.matmul(bank[:, :], hidT[o % 2][:, k, :], slot[:, k, cols], start=False, stop=False)
                        ins = pe.matmul(bank[:, :], hidT[o % 2][:, 3, :], slot[:, 3, cols], start=False, stop=True)
                        ins.then_inc(bk.full_sem(("y", l, o, i)), 1)
                    m.last_use(("down", l, o), ("y", l, o, 1))

        @block.scalar
        def _(act):
            for n in range(nb + 1):
                if n < nb:
                    for i in range(2):
                        act.wait_ge(*bk.made(("xbT", l, n, i)))
                        bank = bk.bank(("xbT", l, n, i))
                        act.activation(xbT[n % 2][:, 4 * i:4 * i + 4, :],
                                                bank[:, :].rearrange("p (a b) -> p a b", a=4), ACT.Copy).then_inc(bk.free_sem(("xbT", l, n, i)), 1)
                if n >= 1:
                    o = n - 1
                    act.wait_ge(*bk.made(("hT", l, o)))
                    bank = bk.bank(("hT", l, o))
                    act.activation(hidT[o % 2], bank[:, :].rearrange("p (a b) -> p a b", a=4), ACT.Copy).then_inc(bk.free_sem(("hT", l, o)), 1)
                if n < nb:
                    act.wait_ge(*bk.made(("g", l, n)))
                    bank = bk.bank(("g", l, n))
                    act.activation(silu[n % 2], bank[:, :], ACT.Silu).then_inc(bk.free_sem(("g", l, n)), 1)

        @block.vector
        def _(dve):
            for n in range(nb + 1):
                if n < nb:
                    dve.wait_ge(*bk.read_done(("g", l, n)))
                    dve.wait_ge(*bk.made(("u", l, n)))
                    bank = bk.bank(("u", l, n))
                    ins = dve.tensor_tensor(hid[n % 2], silu[n % 2], bank[:, :], ALU.mult)
                    ins.then_inc(m.tally("hidden_values").up(), 1)
                    dve.wait_ge(*m.tally("hidden_values").at(n + 1))
                    dve.memset(m.v[:, 41:42], 0.0).then_inc(bk.free_sem(("u", l, n)), 1)
                if n >= 1:
                    o = n - 1
                    if o >= 2:
                        dve.wait_ge(*y_out.at(o - 2))
                    for i in range(2):
                        dve.wait_ge(*bk.made(("y", l, o, i)))
                        bank = bk.bank(("y", l, o, i))
                        dve.tensor_copy(y[o % 2][:, i, :], bank[:, :]).then_inc(bk.free_sem(("y", l, o, i)), 1)

        @block.gpsimd
        def _(pool):
            pool.dma_start(xb[0], m.dram["slots_x"][0:P, :]).then_inc(x_in.of(0), 16)
            for n in range(nb + 1):
                if n + 1 < nb:
                    if n >= 1:
                        pool.wait_ge(*bk.made(("xbT", l, n - 1, 1)))
                    pool.dma_start(xb[(n + 1) % 2], m.dram["slots_x"][(n + 1) * P:(n + 2) * P, :]).then_inc(x_in.of(n + 1), 16)
                if n >= 1:
                    o = n - 1
                    for i in range(2):
                        pool.wait_ge(*bk.read_done(("y", l, o, i)))
                    pool.dma_start(m.dram["slots_y"][o * P:(o + 1) * P, :], y[o % 2]).then_inc(y_out.of(o), 16)
            for o in range(max(0, nb - 2), nb):
                pool.wait_ge(*y_out.at(o))
        m.issue_weights(block)
    x_in.advance(nb)
    y_out.advance(nb)


def if_used(pe, n, used):
    return pe.If(used > 0) if n >= ALWAYS_USED else nullcontext()


class Alternating:

    def __init__(self, sems):
        self.sems, self.base = sems, [0, 0]

    def of(self, n):
        return self.sems[n % 2]

    def at(self, n):
        return self.sems[n % 2], self.base[n % 2] + 16 * (n // 2 + 1)

    def advance(self, n):
        self.base = [self.base[0] + 16 * ((n + 1) // 2), self.base[1] + 16 * (n // 2)]


def combine(m, l):
    bk = m.banks
    g = [m.B[4][:, :, :].rearrange("p (t a) b -> p t (a b)", t=TT), m.B[5][:, :, :].rearrange("p (t a) b -> p t (a b)", t=TT)]
    with m.stage() as block:
        @block.gpsimd
        def _(pool):
            for t in range(TT):
                for i in range(2):
                    pool.indirect_dma_start(g[i][:, t, :], None, m.dram["slots_y"],
                                            bass.IndirectOffsetOnAxis(ap=m.slot[:, i, t:t + 1], axis=0)).then_inc(m.pool_dma, 16)
                    m.pool_n += 16
            pool.wait_ge(m.pool_dma, m.pool_n)
        m.issue_weights(block)
    with m.stage() as block:
        for j in range(KT):
            bk.plan(("fT", l, j))

        @block.vector
        def _(dve):
            for t in range(TT):
                dve.tensor_scalar(g[0][:, t, :], g[0][:, t, :], m.weight[:, 0, t:t + 1], None, ALU.mult).then_inc(m.tally("dve_step").up(), 1)
                dve.wait_ge(*m.tally("dve_step").last())
                dve.scalar_tensor_tensor(g[0][:, t, :], g[1][:, t, :], m.weight[:, 1, t:t + 1],
                                                                  g[0][:, t, :], ALU.mult, ALU.add).then_inc(m.tally("combined_rows").up(), 1)
            for j in range(KT):
                dve.wait_ge(*bk.made(("fT", l, j)))
                bank = bk.bank(("fT", l, j))
                dve.scalar_tensor_tensor(m.B[1][:, j, :], m.XT[:, j, :], ALPHA, bank[:, :], ALU.mult, ALU.add).then_inc(bk.free_sem(("fT", l, j)), 1)

        @block.tensor
        def _(pe):
            pe.wait_ge(*m.tally("combined_rows").at(TT))
            for j in range(KT):
                pe.wait_ge(*bk.vacant(("fT", l, j)))
                bank = bk.bank(("fT", l, j))
                for t in range(TT):
                    ins = pe.transpose(bank[:, t * P:(t + 1) * P], g[0][:, t, j * P:(j + 1) * P], m.c("ident"))
                ins.then_inc(bk.full_sem(("fT", l, j)), 1)
        m.issue_weights(block)


def rms_norm(m, tag, src, finish_tile, sq):
    bk = m.banks
    with m.stage() as block:
        bk.plan(("ms", tag))

        @block.scalar
        def _(act):
            for k in range(KT):
                act.activation(sq[:, k, :], src[:, k, :], ACT.Square).then_inc(m.tally("squares").up(), 1)
            act.wait_ge(*bk.read_done(("ms", tag)))
            act.activation(m.T[0][:, :], m.T[0][:, :], ACT.Sqrt).then_inc(m.tally("roots").up(), 1)

        @block.tensor
        def _(pe):
            pe.wait_ge(*bk.vacant(("ms", tag)))
            bank = bk.bank(("ms", tag))
            for k in range(KT):
                pe.wait_ge(*m.tally("squares").at(k + 1))
                ins = pe.matmul(bank[:, :], m.c("ones_over_d"), sq[:, k, :], start=k == 0, stop=k == KT - 1)
            ins.then_inc(bk.full_sem(("ms", tag)), 1)

        @block.vector
        def _(dve):
            dve.wait_ge(*bk.made(("ms", tag)))
            bank = bk.bank(("ms", tag))
            dve.tensor_scalar(m.T[0][:, :], bank[:, :], 1e-6, None, ALU.add).then_inc(bk.free_sem(("ms", tag)), 1)
            dve.wait_ge(*m.tally("roots").at(1))
            dve.reciprocal(m.T[1][:, :], m.T[0][:, :]).then_inc(m.tally("dve_step").up(), 1)
            dve.wait_ge(*m.tally("dve_step").last())
            for k in range(KT):
                finish_tile(dve, k)
        m.issue_weights(block)


def pre_norm(m, tag, gain):
    def tile(dve, k):
        dve.tensor_tensor(m.B[0][:, k, :], m.XT[:, k, :], m.T[1][:, :], ALU.mult).then_inc(m.tally("dve_step").up(), 1)
        dve.wait_ge(*m.tally("dve_step").last())
        dve.tensor_scalar(m.B[0][:, k, :], m.B[0][:, k, :], m.p(gain, k), None, ALU.mult).then_inc(m.tally("dve_step").up(), 1)
        dve.wait_ge(*m.tally("dve_step").last())
    rms_norm(m, tag, m.XT, tile, m.B[0])


def post_norm(m, tag, src, gain, sq):
    def tile(dve, k):
        dve.tensor_tensor(src[:, k, :], src[:, k, :], m.T[1][:, :], ALU.mult).then_inc(m.tally("dve_step").up(), 1)
        dve.wait_ge(*m.tally("dve_step").last())
        dve.scalar_tensor_tensor(m.XT[:, k, :], src[:, k, :], m.p(gain, k), m.XT[:, k, :], ALU.mult, ALU.add).then_inc(m.tally("dve_step").up(), 1)
        dve.wait_ge(*m.tally("dve_step").last())
    rms_norm(m, tag, src, tile, sq)


def second_projection(m):
    bk = m.banks
    h = lambda k: m.B[0][:, k, :]
    dest = [m.B[1][:, j, :] for j in range(8)] + [m.B[2][:, j, :] for j in range(6)]
    with m.stage() as block:
        for j in range(18):
            bk.plan(("p2", j))

        @block.tensor
        def _(pe):
            for j in range(18):
                name = ("in2", 0, j // 4)
                pe.wait_ge(*m.landed(name))
                project(m, pe, ("p2", j), by512(m.slot_of(name)), j % 4, KT, h)
                if j % 4 == 3 or j == 17:
                    m.last_use(name, ("p2", j))

        @block.scalar
        def _(act):
            for j in range(14):
                act.wait_ge(*bk.made(("p2", j)))
                bank = bk.bank(("p2", j))
                if j >= 4:
                    act.wait_ge(*m.tally("shifted_tile").at(j - 3))
                act.activation(m.B[4][:, j % 4, :], bank[:, :], ACT.Copy).then_inc(bk.free_sem(("p2", j)), 1)
            for j in range(14, 18):
                act.wait_ge(*bk.made(("p2", j)))
                bank = bk.bank(("p2", j))
                act.activation(m.B[3][:, j - 14, :], bank[:, :], ACT.Copy).then_inc(bk.free_sem(("p2", j)), 1)

        @block.vector
        def _(dve):
            for j in range(14):
                dve.wait_ge(*bk.read_done(("p2", j)))
                raw, d = m.B[4][:, j % 4, :], m.B[4][:, 4 + j % 4, :]
                dve.tensor_tensor(d[:, 1:SEQ], raw[:, 0:SEQ - 1], raw[:, 1:SEQ], ALU.subtract)
                dve.tensor_scalar(d[:, 0:1], raw[:, 0:1], -1.0, None, ALU.mult).then_inc(m.tally("dve_step").up(), 1)
                dve.wait_ge(*m.tally("dve_step").last())
                dve.scalar_tensor_tensor(dest[j], d, m.p("shift_mu", j), raw, ALU.mult, ALU.add).then_inc(m.tally("shifted_tile").up(), 1)
        m.issue_weights(block)


def load_second(m):
    with m.stage() as block:
        @block.scalar
        def _(act):
            for dst, src in ((m.B[5][:, 0:2, :], m.dram["lora"]), (m.memT[:, 5:7, :].rearrange("p a b -> p (a b)"), m.dram["rows"][:, 0, :])):
                act.dma_start(dst, src).then_inc(m.loaded, 16)
                m.load_n += 16
            act.wait_ge(m.loaded, m.load_n)
        m.issue_weights(block)


def rwkv_rates(m):
    bk = m.banks
    lora = m.B[5][:, 0:2, :]
    low, gd = m.B[2][:, 4, :], m.B[2][:, 5, :]
    ld, a, g = m.B[3][:, 4:8, :], m.B[4][:, 0:4, :], m.B[4][:, 4:8, :]
    with m.stage() as block:
        for j in range(CT):
            for w in "wag":
                bk.plan(("rate", w, j))

        @block.scalar
        def _(act):
            act.activation(low[0:64, :], low[0:64, :], ACT.Tanh).then_inc(m.tally("rank_values").up(), 1)
            act.activation(gd, gd, ACT.Sigmoid).then_inc(m.tally("rank_values").up(), 1)
            for j in range(CT):
                act.wait_ge(*bk.made(("rate", "w", j)))
                bank = bk.bank(("rate", "w", j))
                act.activation(ld[:, j, :], bank[:, :], ACT.Sigmoid, bias=m.p("w0", j)).then_inc(bk.free_sem(("rate", "w", j)), 1)
                act.wait_ge(*bk.made(("rate", "a", j)))
                bank = bk.bank(("rate", "a", j))
                act.activation(a[:, j, :], bank[:, :], ACT.Sigmoid, bias=m.p("a0", j)).then_inc(bk.free_sem(("rate", "a", j)), 1)
                act.wait_ge(*bk.made(("rate", "g", j)))
                bank = bk.bank(("rate", "g", j))
                act.activation(g[:, j, :], bank[:, :], ACT.Copy).then_inc(bk.free_sem(("rate", "g", j)), 1)

        @block.tensor
        def _(pe):
            pe.wait_ge(*m.tally("rank_values").at(2))
            for j in range(CT):
                cols = slice(j * P, (j + 1) * P)
                for w, wt, x in (("w", lora[0:64, 0, cols], low[0:64, :]), ("a", lora[64:128, 0, cols], low[64:128, :]),
                                 ("g", lora[:, 1, cols], gd)):
                    pe.wait_ge(*bk.vacant(("rate", w, j)))
                    bank = bk.bank(("rate", w, j))
                    pe.matmul(bank[:, :], wt, x, start=True, stop=True).then_inc(bk.full_sem(("rate", w, j)), 1)

        @block.vector
        def _(dve):
            for j in range(CT):
                dve.wait_ge(*bk.read_done(("rate", "w", j)))
                dve.tensor_scalar(ld[:, j, :], ld[:, j, :], -math.exp(-0.5), None, ALU.mult)
        m.issue_weights(block)


def rwkv_keys(m):
    bk = m.banks
    r, k, v = m.B[1][:, 0:4, :], m.B[1][:, 4:8, :], m.B[2][:, 0:4, :]
    a, kk, bonus, tmp = m.B[4][:, 0:4, :], m.B[5][:, 0:4, :], m.B[5][:, 4:8, :], m.B[0]
    with m.stage() as block:
        for j in range(CT):
            bk.plan(("kn", j))
            bk.plan(("bo", j))

        @block.vector
        def _(dve):
            for j in range(CT):
                dve.tensor_scalar(kk[:, j, :], k[:, j, :], m.p("k_k", j), None, ALU.mult).then_inc(m.tally("dve_step").up(), 1)
                dve.wait_ge(*m.tally("dve_step").last())
                dve.tensor_tensor(tmp[:, j, :], kk[:, j, :], kk[:, j, :], ALU.mult).then_inc(m.tally("head_products").up(), 1)
                t = m.T[0][:, :]
                dve.tensor_scalar(t, a[:, j, :], -1.0, m.p("k_a", j), ALU.add, ALU.mult).then_inc(m.tally("dve_step").up(), 1)
                dve.wait_ge(*m.tally("dve_step").last())
                dve.tensor_scalar(t, t, 1.0, None, ALU.add).then_inc(m.tally("dve_step").up(), 1)
                dve.wait_ge(*m.tally("dve_step").last())
                dve.tensor_tensor(k[:, j, :], k[:, j, :], t, ALU.mult).then_inc(m.tally("dve_step").up(), 1)
                dve.wait_ge(*m.tally("dve_step").last())
                dve.tensor_tensor(t, r[:, j, :], k[:, j, :], ALU.mult).then_inc(m.tally("dve_step").up(), 1)
                dve.wait_ge(*m.tally("dve_step").last())
                dve.tensor_scalar(tmp[:, 4 + j, :], t, m.p("r_k", j), None, ALU.mult).then_inc(m.tally("head_products").up(), 1)
            for j in range(CT):
                dve.wait_ge(*bk.made(("bo", j)))
                bank = bk.bank(("bo", j))
                dve.tensor_tensor(bonus[:, j, :], bank[:, :], v[:, j, :], ALU.mult).then_inc(bk.free_sem(("bo", j)), 1)
                dve.wait_ge(*m.tally("roots").at(j + 1))
                dve.tensor_scalar(tmp[:, j, :], tmp[:, j, :], 1e-12, None, ALU.max).then_inc(m.tally("dve_step").up(), 1)
                dve.wait_ge(*m.tally("dve_step").last())
                dve.reciprocal(tmp[:, j, :], tmp[:, j, :]).then_inc(m.tally("dve_step").up(), 1)
                dve.wait_ge(*m.tally("dve_step").last())
                dve.tensor_tensor(kk[:, j, :], kk[:, j, :], tmp[:, j, :], ALU.mult).then_inc(m.tally("dve_step").up(), 1)
                dve.wait_ge(*m.tally("dve_step").last())

        @block.tensor
        def _(pe):
            for j in range(CT):
                pe.wait_ge(*m.tally("head_products").at(2 * j + 1))
                pe.wait_ge(*bk.vacant(("kn", j)))
                bank = bk.bank(("kn", j))
                pe.matmul(bank[:, :], m.c("head_ones"), tmp[:, j, :], start=True, stop=True).then_inc(bk.full_sem(("kn", j)), 1)
                pe.wait_ge(*m.tally("head_products").at(2 * j + 2))
                pe.wait_ge(*bk.vacant(("bo", j)))
                bank = bk.bank(("bo", j))
                pe.matmul(bank[:, :], m.c("head_ones"), tmp[:, 4 + j, :], start=True, stop=True).then_inc(bk.full_sem(("bo", j)), 1)

        @block.scalar
        def _(act):
            for j in range(CT):
                act.wait_ge(*bk.made(("kn", j)))
                bank = bk.bank(("kn", j))
                act.activation(tmp[:, j, :], bank[:, :], ACT.Sqrt).then_inc(bk.free_sem(("kn", j)), 1)
                act.wait_ge(*bk.read_done(("kn", j)))
                act.activation(m.v[:, 42:43], tmp[:, j, 0:1], ACT.Copy).then_inc(m.tally("roots").up(), 1)
        m.issue_weights(block)


def rwkv_scaled(m):
    r, k = m.B[1][:, 0:4, :], m.B[1][:, 4:8, :]
    a, kk, ld = m.B[4][:, 0:4, :], m.B[5][:, 0:4, :], m.B[3][:, 4:8, :]
    reset = m.memT[:, 5:7, :].rearrange("p a b -> p (a b)")
    pc = m.pc
    with m.stage() as block:
        @block.vector
        def _(dve):
            for j in range(CT):
                cl, prev = m.B[0][:, j, :], m.B[0][:, 4 + j, :]
                dve.tensor_tensor_scan(cl, reset, ld[:, j, :], 0.0, ALU.mult, ALU.add).then_inc(m.tally("dve_step").up(), 1)
                dve.wait_ge(*m.tally("dve_step").last())
                dve.tensor_tensor(prev, cl, ld[:, j, :], ALU.subtract).then_inc(m.tally("log_decays").up(), 1)
            for j in range(CT):
                pinv, p, pprev = m.B[2][:, 4 + j, :], m.B[0][:, j, :], m.B[0][:, 4 + j, :]
                dve.wait_ge(*m.tally("decays").at(j + 1))
                dve.tensor_tensor(a[:, j, :], a[:, j, :], kk[:, j, :], ALU.mult).then_inc(m.tally("dve_step").up(), 1)
                dve.wait_ge(*m.tally("dve_step").last())
                dve.tensor_tensor(a[:, j, :], a[:, j, :], pinv, ALU.mult).then_inc(m.tally("dve_step").up(), 1)
                dve.wait_ge(*m.tally("dve_step").last())
                dve.scalar_tensor_tensor(kk[:, j, :], kk[:, j, :], -1.0, pprev, ALU.mult, ALU.mult).then_inc(m.tally("dve_step").up(), 1)
                dve.wait_ge(*m.tally("dve_step").last())
                dve.tensor_tensor(k[:, j, :], k[:, j, :], pinv, ALU.mult).then_inc(m.tally("dve_step").up(), 1)
                dve.wait_ge(*m.tally("dve_step").last())
                dve.tensor_tensor(r[:, j, :], r[:, j, :], p, ALU.mult).then_inc(m.tally("dve_step").up(), 1)
                dve.wait_ge(*m.tally("dve_step").last())
                dve.tensor_copy(pc[:, :, j], p.rearrange("p (c t) -> p c t", t=32)[:, :, 31])
            for i in range(4):
                dve.memset(m.gt[:, i, :, :], 0.0)
                dve.memset(m.sbd[:, i, :, :], 0.0)
            dve.memset(m.state[:, 0, :, :], 0.0)

        @block.scalar
        def _(act):
            for j in range(CT):
                cl, prev, pinv = m.B[0][:, j, :], m.B[0][:, 4 + j, :], m.B[2][:, 4 + j, :]
                act.wait_ge(*m.tally("log_decays").at(j + 1))
                act.activation(pinv, cl, ACT.Exp, scale=-1.0).then_inc(m.tally("act_step").up(), 1)
                act.wait_ge(*m.tally("act_step").last())
                act.activation(cl, cl, ACT.Exp).then_inc(m.tally("act_step").up(), 1)
                act.wait_ge(*m.tally("act_step").last())
                act.activation(prev, prev, ACT.Exp).then_inc(m.tally("decays").up(), 1)
        m.issue_weights(block)


def rwkv_group(m, tg):
    bk = m.banks
    toks = slice(tg * P, (tg + 1) * P)
    A, Bh, Kh, Rh, V = m.B[5][:, 0:4, :], m.B[4][:, 0:4, :], m.B[1][:, 4:8, :], m.B[1][:, 0:4, :], m.B[2][:, 0:4, :]
    B0, B2, B3 = m.B[0], m.B[2], m.B[3]
    tokA, tokB, tokK, tokV = (B0[:, i, :] for i in range(4))
    pair = lambda b, i: b[:, i:i + 2, :].rearrange("p a (c t) -> p a c t", t=P)
    M, MT, TTr = pair(B0, 4), pair(B0, 6), pair(B2, 4)
    MkT, NbT, NkT = pair(B2, 6), pair(B3, 4), pair(B3, 6)
    W1, U = m.w1, m.u1
    Rt = m.rt[:, :].rearrange("p (c t) -> p c t", t=P)
    state, hmat, gt, sbd = m.state, m.hmat, m.gt, m.sbd
    heads = [(par, ct) for par in range(2) for ct in range(4)]
    rows = lambda par: slice(64 * par, 64 * par + 64)
    hcol = lambda par, ct: slice(ct * P + 64 * par, ct * P + 64 * par + 64)
    key = lambda *k: ("rw", tg, *k)

    grams = [("L", A, Bh, M, "chunk_lower"), ("LT", Bh, A, MT, "chunk_upper"), ("MkT", Kh, A, MkT, "chunk_upper"),
             ("NbT", Bh, Rh, NbT, "chunk_upper_incl"), ("NkT", Kh, Rh, NkT, "chunk_upper_incl")]
    with m.stage() as block:
        for i, name in enumerate("ABKV"):
            bk.plan(key("tok", name))
        for g in grams:
            for par in range(2):
                bk.plan(key(g[0], par))

        @block.tensor
        def _(pe):
            for name, src in zip("ABKV", (A, Bh, Kh, V)):
                pe.wait_ge(*bk.vacant(key("tok", name)))
                bank = bk.bank(key("tok", name))
                for ct in range(4):
                    ins = pe.transpose(bank[:, ct * P:(ct + 1) * P], src[:, ct, toks], m.c("ident"))
                ins.then_inc(bk.full_sem(key("tok", name)), 1)
            for name, left, right, _, _ in grams:
                for par in range(2):
                    pe.wait_ge(*bk.vacant(key(name, par)))
                    bank = bk.bank(key(name, par))
                    for ct in range(4):
                        ins = pe.matmul(bank[:, ct * P:(ct + 1) * P], left[rows(par), ct, toks], right[rows(par), ct, toks],
                                        start=True, stop=True)
                    ins.then_inc(bk.full_sem(key(name, par)), 1)

        @block.scalar
        def _(act):
            for name, dst in zip("ABKV", (tokA, tokB, tokK, tokV)):
                act.wait_ge(*bk.made(key("tok", name)))
                bank = bk.bank(key("tok", name))
                act.activation(dst, bank[:, :], ACT.Copy).then_inc(bk.free_sem(key("tok", name)), 1)
            act.wait_ge(*bk.read_done(key("tok", "A")))
            for par in range(2):
                act.activation(W1[:, par, :, 64:128], tokA.rearrange("p (c a v) -> p a c v", a=2, v=64)[:, par], ACT.Copy)

        @block.vector
        def _(dve):
            for name, _, _, dst, mask in grams:
                for par in range(2):
                    dve.wait_ge(*bk.made(key(name, par)))
                    bank = bk.bank(key(name, par))
                    dve.tensor_tensor(dst[:, par], bank[:, :].rearrange("p (c t) -> p c t", t=P),
                                               m.c(mask).unsqueeze(1).broadcast_to([P, 4, P]), ALU.mult).then_inc(bk.free_sem(key(name, par)), 1)
            dve.wait_ge(*bk.read_done(key("LT", 1)))
            for par in range(2):
                dve.tensor_tensor(TTr[:, par], MT[:, par], m.c("ident").unsqueeze(1).broadcast_to([P, 4, P]), ALU.add)
        m.issue_weights(block)

    for step in range(4):
        last = step == 3
        with m.stage() as block:
            for par in range(2):
                bk.plan(key("sq", step, par))
                if not last:
                    bk.plan(key("sqT", step, par))
            if step == 0:
                bk.plan(key("mv"))

            @block.tensor
            def _(pe):
                for par in range(2):
                    pe.wait_ge(*bk.vacant(key("sq", step, par)))
                    bank = bk.bank(key("sq", step, par))
                    for ct in range(4):
                        ins = pe.matmul(bank[:, ct * P:(ct + 1) * P], MT[:, par, ct, :], M[:, par, ct, :], start=True, stop=True)
                    ins.then_inc(bk.full_sem(key("sq", step, par)), 1)
                    if not last:
                        pe.wait_ge(*bk.vacant(key("sqT", step, par)))
                        bank = bk.bank(key("sqT", step, par))
                        for ct in range(4):
                            ins = pe.matmul(bank[:, ct * P:(ct + 1) * P], M[:, par, ct, :], MT[:, par, ct, :], start=True, stop=True)
                        ins.then_inc(bk.full_sem(key("sqT", step, par)), 1)
                if step == 0:
                    pe.wait_ge(*bk.vacant(key("mv")))
                    bank = bk.bank(key("mv"))
                    for i, (par, ct) in enumerate(heads):
                        ins = pe.matmul(bank[:, i * 64:(i + 1) * 64], MkT[:, par, ct, :], tokV[:, hcol(par, ct)], start=True, stop=True)
                    ins.then_inc(bk.full_sem(key("mv")), 1)

            @block.scalar
            def _(act):
                for par in range(2):
                    if not last:
                        act.wait_ge(*bk.made(key("sqT", step, par)))
                    act.wait_ge(*bk.made(key("sq", step, par)))
                    bank = bk.bank(key("sq", step, par))
                    act.activation(M[:, par], bank[:, :].rearrange("p (c t) -> p c t", t=P), ACT.Copy).then_inc(bk.free_sem(key("sq", step, par)), 1)
                if step == 0:
                    act.wait_ge(*bk.made(key("mv")))
                    bank = bk.bank(key("mv"))
                    act.activation(W1[:, :, :, 0:64], bank[:, :].rearrange("p (a c v) -> p a c v", a=2, v=64), ACT.Copy).then_inc(bk.free_sem(key("mv")), 1)

            @block.vector
            def _(dve):
                if not last:
                    for par in range(2):
                        dve.wait_ge(*bk.made(key("sqT", step, par)))
                        bank = bk.bank(key("sqT", step, par))
                        dve.tensor_copy(MT[:, par], bank[:, :].rearrange("p (c t) -> p c t", t=P)).then_inc(bk.free_sem(key("sqT", step, par)), 1)
            m.issue_weights(block)
        with m.stage() as block:
            for par in range(2):
                bk.plan(key("tt", step, par))

            @block.tensor
            def _(pe):
                for par in range(2):
                    pe.wait_ge(*bk.vacant(key("tt", step, par)))
                    bank = bk.bank(key("tt", step, par))
                    for ct in range(4):
                        ins = pe.matmul(bank[:, ct * P:(ct + 1) * P], M[:, par, ct, :], TTr[:, par, ct, :], start=True, stop=True)
                    ins.then_inc(bk.full_sem(key("tt", step, par)), 1)

            @block.vector
            def _(dve):
                for par in range(2):
                    dve.wait_ge(*bk.made(key("tt", step, par)))
                    bank = bk.bank(key("tt", step, par))
                    dve.tensor_tensor(TTr[:, par], TTr[:, par], bank[:, :].rearrange("p (c t) -> p c t", t=P), ALU.add).then_inc(bk.free_sem(key("tt", step, par)), 1)
            m.issue_weights(block)

    with m.stage() as block:
        for par in range(2):
            bk.plan(key("u", par))
        bk.plan(key("rt"))
        for c in range(4):
            bk.plan(key("gh", c))

        @block.tensor
        def _(pe):
            for par in range(2):
                pe.wait_ge(*bk.vacant(key("u", par)))
                bank = bk.bank(key("u", par))
                for ct in range(4):
                    ins = pe.matmul(bank[:, ct * P:(ct + 1) * P], TTr[:, par, ct, :], W1[:, par, ct, :], start=True, stop=True)
                ins.then_inc(bk.full_sem(key("u", par)), 1)
            pe.wait_ge(*bk.read_done(key("u", 0)))
            pe.wait_ge(*bk.read_done(key("u", 1)))
            for c in range(4):
                t = slice(32 * c, 32 * c + 32)
                pe.wait_ge(*bk.vacant(key("gh", c)))
                bank = bk.bank(key("gh", c))
                for par, ct in heads:
                    out = bank[rows(par), ct * 64:ct * 64 + 64]
                    pe.matmul(out, U[t, par, ct, 64:128], tokB[t, hcol(par, ct)], start=True, stop=True)
                    out = bank[rows(par), 256 + ct * 64:256 + ct * 64 + 64]
                    pe.matmul(out, tokB[t, hcol(par, ct)], U[t, par, ct, 0:64], start=True, stop=False)
                    ins = pe.matmul(out, tokK[t, hcol(par, ct)], tokV[t, hcol(par, ct)], start=False, stop=True)
                ins.then_inc(bk.full_sem(key("gh", c)), 1)
            pe.wait_ge(*bk.vacant(key("rt")))
            bank = bk.bank(key("rt"))
            for par, ct in heads:
                ins = pe.matmul(bank[rows(par), ct * P:(ct + 1) * P], U[:, par, ct, 64:128], NbT[:, par, ct, :], start=True, stop=True)
            ins.then_inc(bk.full_sem(key("rt")), 1)

        @block.scalar
        def _(act):
            for par in range(2):
                act.wait_ge(*bk.made(key("u", par)))
                bank = bk.bank(key("u", par))
                act.activation(U[:, par], bank[:, :].rearrange("p (c t) -> p c t", t=P), ACT.Copy).then_inc(bk.free_sem(key("u", par)), 1)
            for c in range(4):
                act.wait_ge(*bk.made(key("gh", c)))
                bank = bk.bank(key("gh", c))
                g = bank[:, 0:256].rearrange("p (c k) -> p c k", k=64)
                act.activation(gt[0:64, c, :, 0:64], g[0:64], ACT.Copy)
                act.activation(gt[64:128, c, :, 64:128], g[64:128], ACT.Copy).then_inc(m.tally("act_step").up(), 1)
                act.wait_ge(*m.tally("act_step").last())
                act.activation(hmat[:, c, :, :], bank[:, 256:512].rearrange("p (c k) -> p c k", k=64), ACT.Copy).then_inc(bk.free_sem(key("gh", c)), 1)

        @block.vector
        def _(dve):
            dve.wait_ge(*bk.made(key("rt")))
            bank = bk.bank(key("rt"))
            dve.tensor_tensor(Rt, bank[:, :].rearrange("p (c t) -> p c t", t=P), Rh[:, :, toks], ALU.add).then_inc(bk.free_sem(key("rt")), 1)
        m.issue_weights(block)

    with m.stage() as block:
        for c in range(4):
            bk.plan(key("s", c))
        bk.plan(key("y"))
        step_ready, sbd_ready = m.tally("chunk_state"), m.tally("paired_state")

        @block.tensor
        def _(pe):
            for c in range(4):
                if c:
                    pe.wait_ge(*step_ready.at(c))
                pe.wait_ge(*bk.vacant(key("s", c)))
                bank = bk.bank(key("s", c))
                for ct in range(4):
                    ins = pe.matmul(bank[:, ct * 64:ct * 64 + 64], gt[:, c, ct, :], state[:, c, ct, :], start=True, stop=True)
                ins.then_inc(bk.full_sem(key("s", c)), 1)
            pe.wait_ge(*bk.vacant(key("y")))
            bank = bk.bank(key("y"))
            pe.wait_ge(*sbd_ready.at(4))
            for ct in range(4):
                for par in range(2):
                    out = bank[rows(par), ct * P:(ct + 1) * P]
                    pe.matmul(out, U[:, par, ct, 0:64], NbT[:, par, ct, :], start=True, stop=False)
                    pe.matmul(out, tokV[:, hcol(par, ct)], NkT[:, par, ct, :], start=False, stop=True)
                for c in range(4):
                    cols = slice(ct * P + 32 * c, ct * P + 32 * c + 32)
                    ins = pe.matmul(bank[:, cols], sbd[:, c, ct, :], Rt[:, ct, 32 * c:32 * c + 32], start=False, stop=False,
                                    skip_group_check=True)
            ins.then_inc(bk.full_sem(key("y")), 1)

        @block.vector
        def _(dve):
            for c in range(4):
                dve.tensor_tensor(hmat[:, c], hmat[:, c], state[:, c], ALU.add).then_inc(m.tally("dve_step").up(), 1)
                dve.wait_ge(*m.tally("dve_step").last())
                dve.wait_ge(*bk.made(key("s", c)))
                bank = bk.bank(key("s", c))
                dve.tensor_tensor(hmat[:, c], hmat[:, c], bank[:, 0:256].rearrange("p (c v) -> p c v", v=64), ALU.add).then_inc(bk.free_sem(key("s", c)), 1)
                dve.wait_ge(*bk.read_done(key("s", c)))
                dve.tensor_tensor(state[:, c + 1], hmat[:, c],
                                                 m.pc[:, 4 * tg + c, :].unsqueeze(2).broadcast_to([P, 4, 64]), ALU.mult).then_inc(step_ready.up(), 1)
                dve.wait_ge(*step_ready.at(c + 1))
            dve.wait_ge(*bk.made(key("y")))
            bank = bk.bank(key("y"))
            dve.tensor_copy(state[:, 0], state[:, 4])
            dve.tensor_copy(Rh[:, :, toks], bank[:, :].rearrange("p (c t) -> p c t", t=P)).then_inc(bk.free_sem(key("y")), 1)

        @block.scalar
        def _(act):
            for c in range(4):
                if c:
                    act.wait_ge(*step_ready.at(c))
                act.activation(sbd[0:64, c, :, 0:64], state[0:64, c], ACT.Copy)
                act.activation(sbd[64:128, c, :, 64:128], state[64:128, c], ACT.Copy).then_inc(sbd_ready.up(), 1)
        m.issue_weights(block)


def rwkv_output(m):
    bk = m.banks
    y, g, bonus = m.B[1][:, 0:4, :], m.B[4][:, 4:8, :], m.B[5][:, 4:8, :]
    sq, rstd = m.B[0][:, 0:4, :], m.B[0][:, 4:8, :]
    with m.stage() as block:
        for j in range(CT):
            bk.plan(("gm", j))
        for j in range(CT):
            bk.plan(("gv", j))

        @block.tensor
        def _(pe):
            for j in range(CT):
                pe.wait_ge(*bk.vacant(("gm", j)))
                bank = bk.bank(("gm", j))
                pe.matmul(bank[:, :], m.c("head_ones"), y[:, j, :], start=True, stop=True).then_inc(bk.full_sem(("gm", j)), 1)
            for j in range(CT):
                pe.wait_ge(*m.tally("squares").at(j + 1))
                pe.wait_ge(*bk.vacant(("gv", j)))
                bank = bk.bank(("gv", j))
                pe.matmul(bank[:, :], m.c("head_ones"), sq[:, j, :], start=True, stop=True).then_inc(bk.full_sem(("gv", j)), 1)

        @block.vector
        def _(dve):
            for j in range(CT):
                dve.wait_ge(*bk.made(("gm", j)))
                bank = bk.bank(("gm", j))
                dve.scalar_tensor_tensor(y[:, j, :], bank[:, :], -1.0 / 64, y[:, j, :], ALU.mult, ALU.add).then_inc(bk.free_sem(("gm", j)), 1)
            for j in range(CT):
                dve.wait_ge(*bk.made(("gv", j)))
                bank = bk.bank(("gv", j))
                dve.tensor_scalar(rstd[:, j, :], bank[:, :], 1.0 / 64, 64e-5, ALU.mult, ALU.add).then_inc(bk.free_sem(("gv", j)), 1)
            for j in range(CT):
                dve.wait_ge(*m.tally("roots").at(j + 1))
                dve.reciprocal(rstd[:, j, :], rstd[:, j, :]).then_inc(m.tally("dve_step").up(), 1)
                dve.wait_ge(*m.tally("dve_step").last())
                dve.tensor_tensor(y[:, j, :], y[:, j, :], rstd[:, j, :], ALU.mult).then_inc(m.tally("dve_step").up(), 1)
                dve.wait_ge(*m.tally("dve_step").last())
                dve.tensor_scalar(y[:, j, :], y[:, j, :], m.p("lnx_w", j), m.p("lnx_b", j), ALU.mult, ALU.add).then_inc(m.tally("dve_step").up(), 1)
                dve.wait_ge(*m.tally("dve_step").last())
                dve.tensor_tensor(y[:, j, :], y[:, j, :], bonus[:, j, :], ALU.add).then_inc(m.tally("dve_step").up(), 1)
                dve.wait_ge(*m.tally("dve_step").last())
                dve.tensor_tensor(y[:, j, :], y[:, j, :], g[:, j, :], ALU.mult)

        @block.scalar
        def _(act):
            for j in range(CT):
                act.wait_ge(*bk.read_done(("gm", j)))
                act.activation(sq[:, j, :], y[:, j, :], ACT.Square).then_inc(m.tally("squares").up(), 1)
            for j in range(CT):
                act.wait_ge(*bk.read_done(("gv", j)))
                act.activation(rstd[:, j, :], rstd[:, j, :], ACT.Sqrt).then_inc(m.tally("roots").up(), 1)
        m.issue_weights(block)


def s5_constants(m):
    V = m.B[4][:, 0, :]
    col = lambda i: V[:, 16 * i:16 * i + 16]
    dt, th, k, f, s, sh, c, den, nr, ni, cfr, cfi, t1, t2, mag = (col(i) for i in range(15))
    re, im, step = m.p("s5_re"), m.p("s5_im"), m.p("s5_step")
    cfull = m.B[5][:, 2:4, :].rearrange("p a (s c) -> p a s c", c=32)
    cnew = m.B[5][:, 4:6, :].rearrange("p a (s c) -> p a s c", c=32)
    tmp = m.B[5][:, 6, :].rearrange("p (s c) -> p s c", c=32)
    with m.stage() as block:
        @block.scalar
        def _(act):
            for dst, src in ((m.B[5][:, 0:2, :].rearrange("p a (b c) -> p a b c", c=P), m.dram["s5_b"]), (cfull, m.dram["s5_c"]),
                             (m.memT[:, 0:2, :].rearrange("p a b -> p (a b)"), m.dram["rows"][:, 1, :]),
                             (m.B[2][:, 4:8, :], m.dram["w_glu"])):
                act.dma_start(dst, src).then_inc(m.loaded, 16)
                m.load_n += 16
            act.activation(dt, step, ACT.Exp).then_inc(m.tally("s5_prepared").up(), 1)
            act.wait_ge(*m.tally("s5_angles").at(1))
            act.activation(m.rho[:, :], t1, ACT.Exp).then_inc(m.tally("s5_prepared").up(), 1)
            act.activation(s, t2, ACT.Sin)
            act.activation(sh, t2, ACT.Sin, scale=0.5).then_inc(m.tally("s5_prepared").up(), 1)
            act.wait_ge(m.loaded, m.load_n)
            act.activation(m.v[:, 43:44], V[:, 0:1], ACT.Copy).then_inc(m.tally("s5_prepared").up(), 1)

        @block.vector
        def _(dve):
            dve.wait_ge(*m.tally("s5_prepared").at(1))
            dve.tensor_tensor(t1, re, dt, ALU.mult).then_inc(m.tally("dve_step").up(), 1)
            dve.wait_ge(*m.tally("dve_step").last())
            dve.tensor_tensor(th, im, dt, ALU.mult).then_inc(m.tally("dve_step").up(), 1)
            dve.wait_ge(*m.tally("dve_step").last())
            dve.tensor_scalar(f, th, 1.0 / (2 * math.pi), None, ALU.mult).then_inc(m.tally("dve_step").up(), 1)
            dve.wait_ge(*m.tally("dve_step").last())
            dve.tensor_scalar(k, f, MAGIC, None, ALU.add).then_inc(m.tally("dve_step").up(), 1)
            dve.wait_ge(*m.tally("dve_step").last())
            dve.tensor_scalar(k, k, -MAGIC, None, ALU.add).then_inc(m.tally("dve_step").up(), 1)
            dve.wait_ge(*m.tally("dve_step").last())
            dve.tensor_copy(t2, th).then_inc(m.tally("dve_step").up(), 1)
            dve.wait_ge(*m.tally("dve_step").last())
            for part in (TWO_PI_1, TWO_PI_2, TWO_PI_3):
                dve.scalar_tensor_tensor(t2, k, -part, t2, ALU.mult, ALU.add).then_inc(m.tally("dve_step").up(), 1)
                dve.wait_ge(*m.tally("dve_step").last())
            dve.tensor_scalar(t2, t2, 3.1415925, -3.1415925, ALU.min, ALU.max).then_inc(m.tally("s5_angles").up(), 1)
            dve.wait_ge(*m.tally("s5_angles").at(1))
            dve.tensor_scalar(f, t2, 1.0 / (2 * math.pi), None, ALU.mult).then_inc(m.tally("dve_step").up(), 1)
            dve.wait_ge(*m.tally("dve_step").last())
            dve.tensor_scalar(k, f, 6144.0, None, ALU.add).then_inc(m.tally("dve_step").up(), 1)
            dve.wait_ge(*m.tally("dve_step").last())
            dve.tensor_scalar(m.f_short[:, :], k, -6144.0, None, ALU.add).then_inc(m.tally("dve_step").up(), 1)
            dve.wait_ge(*m.tally("dve_step").last())
            dve.tensor_tensor(m.f_small[:, :], f, m.f_short[:, :], ALU.subtract).then_inc(m.tally("dve_step").up(), 1)
            dve.wait_ge(*m.tally("dve_step").last())
            dve.wait_ge(*m.tally("s5_prepared").at(3))
            dve.tensor_tensor(c, sh, sh, ALU.mult).then_inc(m.tally("dve_step").up(), 1)
            dve.wait_ge(*m.tally("dve_step").last())
            dve.tensor_scalar(c, c, -2.0, 1.0, ALU.mult, ALU.add).then_inc(m.tally("dve_step").up(), 1)
            dve.wait_ge(*m.tally("dve_step").last())
            dve.tensor_tensor(nr, m.rho[:, :], c, ALU.mult).then_inc(m.tally("dve_step").up(), 1)
            dve.wait_ge(*m.tally("dve_step").last())
            dve.tensor_scalar(nr, nr, -1.0, None, ALU.add).then_inc(m.tally("dve_step").up(), 1)
            dve.wait_ge(*m.tally("dve_step").last())
            dve.tensor_tensor(ni, m.rho[:, :], s, ALU.mult).then_inc(m.tally("dve_step").up(), 1)
            dve.wait_ge(*m.tally("dve_step").last())
            dve.tensor_tensor(den, re, re, ALU.mult).then_inc(m.tally("dve_step").up(), 1)
            dve.wait_ge(*m.tally("dve_step").last())
            dve.tensor_tensor(t1, im, im, ALU.mult).then_inc(m.tally("dve_step").up(), 1)
            dve.wait_ge(*m.tally("dve_step").last())
            dve.tensor_tensor(den, den, t1, ALU.add).then_inc(m.tally("dve_step").up(), 1)
            dve.wait_ge(*m.tally("dve_step").last())
            dve.reciprocal(den, den).then_inc(m.tally("dve_step").up(), 1)
            dve.wait_ge(*m.tally("dve_step").last())
            for out, x, y, op in ((cfr, nr, ni, ALU.add), (cfi, ni, nr, ALU.subtract)):
                dve.tensor_tensor(t1, x, re, ALU.mult).then_inc(m.tally("dve_step").up(), 1)
                dve.wait_ge(*m.tally("dve_step").last())
                dve.tensor_tensor(t2, y, im, ALU.mult).then_inc(m.tally("dve_step").up(), 1)
                dve.wait_ge(*m.tally("dve_step").last())
                dve.tensor_tensor(out, t1, t2, op).then_inc(m.tally("dve_step").up(), 1)
                dve.wait_ge(*m.tally("dve_step").last())
                dve.tensor_tensor(out, out, den, ALU.mult).then_inc(m.tally("dve_step").up(), 1)
                dve.wait_ge(*m.tally("dve_step").last())
            dve.wait_ge(*m.tally("s5_prepared").at(4))
            b = lambda x: x.unsqueeze(2).broadcast_to([P, 16, 32])
            dve.tensor_tensor(cnew[:, 0], cfull[:, 0], b(cfr), ALU.mult).then_inc(m.tally("dve_step").up(), 1)
            dve.wait_ge(*m.tally("dve_step").last())
            dve.tensor_tensor(tmp, cfull[:, 1], b(cfi), ALU.mult).then_inc(m.tally("dve_step").up(), 1)
            dve.wait_ge(*m.tally("dve_step").last())
            dve.tensor_tensor(cnew[:, 0], cnew[:, 0], tmp, ALU.subtract).then_inc(m.tally("dve_step").up(), 1)
            dve.wait_ge(*m.tally("dve_step").last())
            dve.tensor_tensor(cnew[:, 1], cfull[:, 0], b(cfi), ALU.mult).then_inc(m.tally("dve_step").up(), 1)
            dve.wait_ge(*m.tally("dve_step").last())
            dve.tensor_tensor(tmp, cfull[:, 1], b(cfr), ALU.mult).then_inc(m.tally("dve_step").up(), 1)
            dve.wait_ge(*m.tally("dve_step").last())
            dve.scalar_tensor_tensor(cnew[:, 1], cnew[:, 1], -1.0, tmp, ALU.mult, ALU.subtract)
        m.issue_weights(block)


def s5_states(m):
    bk = m.banks
    u = m.B[3][:, 0:4, :]
    bmat = m.B[5][:, 0:2, :].rearrange("p a (b c) -> p a b c", c=P)
    cmat = m.B[5][:, 4:6, :].rearrange("p a (s c) -> p a s c", c=32)
    t_row = m.memT[:, 0:2, :].rearrange("p a b -> p (a b)")
    q = [m.T[0], m.T[1]]
    kk = m.T[2]
    sn = [m.B[0][:, 0, :], m.B[0][:, 1, :]]
    cs = [m.B[0][:, 2, :], m.B[0][:, 3, :]]
    vr, vi, t1 = m.B[0][:, 4, :], m.B[0][:, 5, :], m.B[0][:, 6, :]
    xr = [m.B[4][:, 1, :], m.B[4][:, 2, :]]
    xi = [m.B[4][:, 3, :], m.B[4][:, 4, :]]
    y = m.B[3][:, 4:8, :]
    n_s = 16
    with m.stage() as block:
        for s in range(n_s):
            for p in range(2):
                bk.plan(("bu", s, p), (s % 2) * 2 + p)
        for c in range(4):
            bk.plan(("sy", c), 4 + c)

        @block.tensor
        def _(pe):
            def outputs(s):
                pe.wait_ge(*m.tally("s5_frames").at(s + 1))
                if s % 4 == 0:
                    pe.wait_ge(*bk.vacant(("sy", s // 4)))
                bank = bk.bank(("sy", s // 4))
                rows = slice(32 * (s % 4), 32 * (s % 4) + 32)
                pe.matmul(bank[rows, :], cmat[:, 0, s, :], xr[s % 2], start=True, stop=False)
                ins = pe.matmul(bank[rows, :], cmat[:, 1, s, :], xi[s % 2], start=False, stop=True)
                if s % 4 == 3:
                    ins.then_inc(bk.full_sem(("sy", s // 4)), 1)
                else:
                    ins.then_inc(m.tally("s5_outputs").up(), 1)

            for s in range(n_s + 1):
                if s < n_s:
                    rows = slice(32 * (s % 4), 32 * (s % 4) + 32)
                    for p in range(2):
                        pe.wait_ge(*bk.vacant(("bu", s, p)))
                        bank = bk.bank(("bu", s, p))
                        pe.matmul(bank[:, :], bmat[rows, p, s // 4, :], u[rows, s // 4, :], start=True, stop=True).then_inc(bk.full_sem(("bu", s, p)), 1)
                if s >= 1:
                    outputs(s - 1)

        def outputs_done(eng, s):
            if s % 4 == 3:
                eng.wait_ge(*bk.made(("sy", s // 4)))
            else:
                eng.wait_ge(*m.tally("s5_outputs").at(s - s // 4 + 1))

        @block.vector
        def _(dve):

            def turns(s):
                fs, fl = m.f_short[:, s:s + 1], m.f_small[:, s:s + 1]
                if s >= 2:
                    dve.wait_ge(*m.tally("s5_sines").at(s - 1))
                dve.tensor_scalar(kk[:, :], t_row, fs, MAGIC, ALU.mult, ALU.add).then_inc(m.tally("dve_step").up(), 1)
                dve.wait_ge(*m.tally("dve_step").last())
                dve.tensor_scalar(kk[:, :], kk[:, :], -MAGIC, None, ALU.add).then_inc(m.tally("dve_step").up(), 1)
                dve.wait_ge(*m.tally("dve_step").last())
                dve.scalar_tensor_tensor(q[s % 2][:, :], t_row, fs, kk[:, :], ALU.mult, ALU.subtract).then_inc(m.tally("dve_step").up(), 1)
                dve.wait_ge(*m.tally("dve_step").last())
                dve.scalar_tensor_tensor(q[s % 2][:, :], t_row, fl, q[s % 2][:, :], ALU.mult, ALU.add).then_inc(m.tally("dve_step").up(), 1)
                dve.wait_ge(*m.tally("dve_step").last())
                dve.tensor_scalar(kk[:, :], q[s % 2][:, :], MAGIC, None, ALU.add).then_inc(m.tally("dve_step").up(), 1)
                dve.wait_ge(*m.tally("dve_step").last())
                dve.tensor_scalar(kk[:, :], kk[:, :], -MAGIC, None, ALU.add).then_inc(m.tally("dve_step").up(), 1)
                dve.wait_ge(*m.tally("dve_step").last())
                dve.tensor_tensor(q[s % 2][:, :], q[s % 2][:, :], kk[:, :], ALU.subtract).then_inc(m.tally("dve_step").up(), 1)
                dve.wait_ge(*m.tally("dve_step").last())
                dve.tensor_scalar(q[s % 2][:, :], q[s % 2][:, :], 0.4999999, -0.4999999, ALU.min, ALU.max).then_inc(m.tally("s5_turns").up(), 1)

            turns(0)
            for s in range(n_s):
                if s + 1 < n_s:
                    turns(s + 1)
                b = s % 2
                dve.wait_ge(*m.tally("s5_sines").at(s + 1))
                dve.tensor_scalar(cs[b], cs[b], -2.0, 1.0, ALU.mult, ALU.add).then_inc(m.tally("dve_step").up(), 1)
                dve.wait_ge(*m.tally("dve_step").last())
                dve.wait_ge(*bk.made(("bu", s, 0)))
                re = bk.bank(("bu", s, 0))
                dve.wait_ge(*bk.made(("bu", s, 1)))
                im = bk.bank(("bu", s, 1))
                dve.tensor_tensor(vr, re[:, :], cs[b], ALU.mult).then_inc(m.tally("dve_step").up(), 1)
                dve.wait_ge(*m.tally("dve_step").last())
                dve.tensor_tensor(t1, im[:, :], sn[b], ALU.mult).then_inc(m.tally("dve_step").up(), 1)
                dve.wait_ge(*m.tally("dve_step").last())
                dve.tensor_tensor(vr, vr, t1, ALU.add).then_inc(m.tally("dve_step").up(), 1)
                dve.wait_ge(*m.tally("dve_step").last())
                dve.tensor_tensor(t1, re[:, :], sn[b], ALU.mult).then_inc(bk.free_sem(("bu", s, 0)), 1)
                dve.tensor_tensor(vi, im[:, :], cs[b], ALU.mult).then_inc(bk.free_sem(("bu", s, 1)), 1)
                dve.wait_ge(*bk.read_done(("bu", s, 1)))
                dve.tensor_tensor(vi, vi, t1, ALU.subtract).then_inc(m.tally("dve_step").up(), 1)
                dve.wait_ge(*m.tally("dve_step").last())
                rho = m.rho[:, s:s + 1].broadcast_to([P, SEQ])
                dve.tensor_tensor_scan(vr, rho, vr, 0.0, ALU.mult, ALU.add).then_inc(m.tally("dve_step").up(), 1)
                dve.wait_ge(*m.tally("dve_step").last())
                dve.tensor_tensor_scan(vi, rho, vi, 0.0, ALU.mult, ALU.add).then_inc(m.tally("dve_step").up(), 1)
                dve.wait_ge(*m.tally("dve_step").last())
                if s >= 2:
                    outputs_done(dve, s - 2)
                dve.tensor_tensor(xr[b], vr, cs[b], ALU.mult).then_inc(m.tally("dve_step").up(), 1)
                dve.wait_ge(*m.tally("dve_step").last())
                dve.tensor_tensor(t1, vi, sn[b], ALU.mult).then_inc(m.tally("dve_step").up(), 1)
                dve.wait_ge(*m.tally("dve_step").last())
                dve.tensor_tensor(xr[b], xr[b], t1, ALU.subtract).then_inc(m.tally("dve_step").up(), 1)
                dve.wait_ge(*m.tally("dve_step").last())
                dve.tensor_tensor(xi[b], vr, sn[b], ALU.mult).then_inc(m.tally("dve_step").up(), 1)
                dve.wait_ge(*m.tally("dve_step").last())
                dve.tensor_tensor(t1, vi, cs[b], ALU.mult).then_inc(m.tally("dve_step").up(), 1)
                dve.wait_ge(*m.tally("dve_step").last())
                dve.tensor_tensor(xi[b], xi[b], t1, ALU.add).then_inc(m.tally("s5_frames").up(), 1)
                dve.wait_ge(*m.tally("s5_frames").at(s + 1))
            for c in range(4):
                dve.wait_ge(*bk.made(("sy", c)))
                bank = bk.bank(("sy", c))
                dve.scalar_tensor_tensor(y[:, c, :], u[:, c, :], m.p("s5_d", c), bank[:, :], ALU.mult, ALU.add).then_inc(bk.free_sem(("sy", c)), 1)

        @block.scalar
        def _(act):
            for s in range(n_s):
                b = s % 2
                act.wait_ge(*m.tally("s5_turns").at(s + 1))
                if s >= 2:
                    act.wait_ge(*m.tally("s5_frames").at(s - 1))
                act.activation(sn[b], q[b][:, :], ACT.Sin, scale=2 * math.pi)
                act.activation(cs[b], q[b][:, :], ACT.Sin, scale=math.pi).then_inc(m.tally("act_step").up(), 1)
                act.wait_ge(*m.tally("act_step").last())
                act.activation(cs[b], cs[b], ACT.Square).then_inc(m.tally("s5_sines").up(), 1)
            for c in range(4):
                act.wait_ge(*bk.read_done(("sy", c)))
                act.activation(y[:, c, :], y[:, c, :], ACT.Gelu_apprx_tanh)
        m.issue_weights(block)


def s5_glu(m):
    bk = m.banks
    y, w = m.B[3][:, 4:8, :], m.B[2][:, 4:8, :]
    with m.stage() as block:
        for j in range(CT):
            bk.plan(("glu", j))

        @block.tensor
        def _(pe):
            for j in range(CT):
                project(m, pe, ("glu", j), lambda k, c: w[:, k, c * P:(c + 1) * P], j, CT, lambda k: y[:, k, :])

        @block.scalar
        def _(act):
            for j in range(CT):
                act.wait_ge(*bk.made(("glu", j)))
                bank = bk.bank(("glu", j))
                act.activation(m.B[3][:, j, :], bank[:, :], ACT.Sigmoid, bias=m.p("b_glu", j)).then_inc(bk.free_sem(("glu", j)), 1)

        @block.vector
        def _(dve):
            for j in range(CT):
                dve.wait_ge(*bk.read_done(("glu", j)))
                dve.tensor_tensor(m.B[3][:, j, :], m.B[3][:, j, :], y[:, j, :], ALU.mult)
        m.issue_weights(block)


def second_merge(m):
    bk = m.banks
    merged, sig = m.B[4], m.B[5]
    h = lambda k: m.B[0][:, k, :]
    rhs = [lambda k: m.B[1][:, k, :], lambda k: m.B[3][:, k, :]]
    jobs = [(b, j) for b in range(2) for j in range(KT)]
    with m.stage() as block:
        for b, j in jobs:
            bk.plan(("gate2", b, j))
            bk.plan(("branch2", b, j))

        @block.tensor
        def _(pe):
            for b, j in jobs:
                g = ("in2", 0, 5 + 2 * b + j // 4)
                pe.wait_ge(*m.landed(g))
                project(m, pe, ("gate2", b, j), by512(m.slot_of(g)), j % 4, KT, h)
                if j % 4 == 3:
                    m.last_use(g, ("gate2", b, j))
                w = (("br_rwkv", "br_s5")[b], 0, 0)
                pe.wait_ge(*m.landed(w))
                project(m, pe, ("branch2", b, j), by1024(m.slot_of(w)), j, CT, rhs[b])
                if j == KT - 1:
                    m.last_use(w, ("branch2", b, j))

        @block.scalar
        def _(act):
            for i, (b, j) in enumerate(jobs):
                act.wait_ge(*bk.made(("gate2", b, j)))
                bank = bk.bank(("gate2", b, j))
                if i >= 4:
                    act.wait_ge(*bk.read_done(("branch2", *jobs[i - 4])))
                act.activation(sig[:, i % 4, :], bank[:, :], ACT.Sigmoid, bias=m.p("b_gate", 8 * b + j)).then_inc(bk.free_sem(("gate2", b, j)), 1)

        @block.vector
        def _(dve):
            for i, (b, j) in enumerate(jobs):
                dve.wait_ge(*bk.read_done(("gate2", b, j)))
                dve.wait_ge(*bk.made(("branch2", b, j)))
                bank = bk.bank(("branch2", b, j))
                if b == 0:
                    dve.tensor_tensor(merged[:, j, :], bank[:, :], sig[:, i % 4, :], ALU.mult).then_inc(bk.free_sem(("branch2", b, j)), 1)
                    continue
                t = sig[:, 4 + i % 4, :]
                dve.tensor_tensor(t, bank[:, :], sig[:, i % 4, :], ALU.mult).then_inc(bk.free_sem(("branch2", b, j)), 1)
                dve.wait_ge(*bk.read_done(("branch2", b, j)))
                dve.tensor_tensor(merged[:, j, :], merged[:, j, :], t, ALU.add).then_inc(m.tally("dve_step").up(), 1)
                dve.wait_ge(*m.tally("dve_step").last())
        m.issue_weights(block)


def second_out(m):
    bk = m.banks
    with m.stage() as block:
        for j in range(KT):
            bk.plan(("mix2", j))

        @block.tensor
        def _(pe):
            for j in range(KT):
                name = ("out2", 0, j // 4)
                pe.wait_ge(*m.landed(name))
                project(m, pe, ("mix2", j), by512(m.slot_of(name)), j % 4, KT, lambda k: m.B[4][:, k, :])
                if j % 4 == 3:
                    m.last_use(name, ("mix2", j))

        @block.vector
        def _(dve):
            for j in range(KT):
                dve.wait_ge(*bk.made(("mix2", j)))
                bank = bk.bank(("mix2", j))
                dve.tensor_copy(m.B[1][:, j, :], bank[:, :]).then_inc(bk.free_sem(("mix2", j)), 1)
        m.issue_weights(block)


def hidden_tile(m, j):
    return m.B[2 + j // 8][:, j % 8, :]


def ffn_up(m):
    bk = m.banks
    h = lambda k: m.B[0][:, k, :]
    z = [m.B[5][:, i, :] for i in range(4)]
    y = [m.B[5][:, 4 + i, :] for i in range(4)]
    order = [(j, i) for j in range(FF_T // 2) for i in range(2)]
    tiles = [(j, i, p) for j, i in order for p in range(2)]
    with m.stage() as block:
        for t in tiles:
            bk.plan(("ff", *t))

        @block.tensor
        def _(pe):
            for j, i, p in tiles:
                pe.wait_ge(*m.landed(("ffn_up", 0, j)))
                project(m, pe, ("ff", j, i, p), by512(m.slot_of(("ffn_up", 0, j))), 2 * p + i, KT, h)
                if (i, p) == (1, 1):
                    m.last_use(("ffn_up", 0, j), ("ff", j, i, p))

        def gelu(act, n):
            act.wait_ge(*m.tally("convolved").at(n + 1))
            act.activation(y[n % 4], y[n % 4], ACT.Gelu_apprx_tanh).then_inc(m.tally("gelu_done").up(), 1)

        @block.scalar
        def _(act):
            for n, (j, i, p) in enumerate(tiles):
                act.wait_ge(*bk.made(("ff", j, i, p)))
                bank = bk.bank(("ff", j, i, p))
                if n >= 4:
                    act.wait_ge(*m.tally("convolved").at(n - 3))
                act.activation(z[n % 4], bank[:, :], ACT.Copy).then_inc(bk.free_sem(("ff", j, i, p)), 1)
                if p == 1:
                    gelu(act, n - 1)

        @block.vector
        def _(dve):
            for n, (j, i, p) in enumerate(tiles):
                col = 2 * j + i + FF_T * p
                w = lambda tap: m.p("ffn_conv_w", tap * 2 * FF_T + col)
                dve.wait_ge(*bk.read_done(("ff", j, i, p)))
                dve.tensor_scalar(y[n % 4], z[n % 4], w(2), m.p("ffn_conv_b", col), ALU.mult, ALU.add).then_inc(m.tally("dve_step").up(), 1)
                dve.wait_ge(*m.tally("dve_step").last())
                dve.scalar_tensor_tensor(y[n % 4][:, 1:SEQ], z[n % 4][:, 0:SEQ - 1], w(1), y[n % 4][:, 1:SEQ], ALU.mult, ALU.add).then_inc(m.tally("dve_step").up(), 1)
                dve.wait_ge(*m.tally("dve_step").last())
                dve.scalar_tensor_tensor(y[n % 4][:, 2:SEQ], z[n % 4][:, 0:SEQ - 2], w(0), y[n % 4][:, 2:SEQ], ALU.mult, ALU.add).then_inc(m.tally("convolved").up(), 1)
                if p == 1:
                    dve.wait_ge(*m.tally("convolved").at(n + 1))
                    dve.wait_ge(*m.tally("gelu_done").at(n // 2 + 1))
                    dve.tensor_tensor(hidden_tile(m, 2 * j + i), y[(n - 1) % 4], y[n % 4], ALU.mult).then_inc(m.tally("dve_step").up(), 1)
                    dve.wait_ge(*m.tally("dve_step").last())
        m.issue_weights(block)


def ffn_down(m):
    bk = m.banks
    with m.stage() as block:
        for c in range(KT):
            bk.plan(("fd", c))

        @block.tensor
        def _(pe):
            for k in range(FF_T):
                name = ("ffn_down", 0, k // 4)
                pe.wait_ge(*m.landed(name))
                slot = by1024(m.slot_of(name))
                for c in range(KT):
                    if k == 0:
                        pe.wait_ge(*bk.vacant(("fd", c)))
                    bank = bk.bank(("fd", c))
                    ins = pe.matmul(bank[:, :], slot(k % 4, c), hidden_tile(m, k), start=k == 0, stop=k == FF_T - 1)
                    if k == FF_T - 1:
                        ins.then_inc(bk.full_sem(("fd", c)), 1)
                if k % 4 == 3:
                    used = m.tally("chunk_used")
                    ins.then_inc(used.up(), 1)
                    m.last_uses[m.index[name]] = (used.sem, used.made)

        @block.vector
        def _(dve):
            for c in range(KT):
                dve.wait_ge(*bk.made(("fd", c)))
                bank = bk.bank(("fd", c))
                dve.tensor_copy(m.B[1][:, c, :], bank[:, :]).then_inc(bk.free_sem(("fd", c)), 1)
        m.issue_weights(block)


def second_stages(m):
    yield lambda: load_second(m)
    yield lambda: pre_norm(m, "mix_pre", "norm_mix_pre")
    yield lambda: second_projection(m)
    yield lambda: spill_x(m)
    yield lambda: rwkv_rates(m)
    yield lambda: rwkv_keys(m)
    yield lambda: rwkv_scaled(m)
    for tg in range(TT):
        yield lambda: rwkv_group(m, tg)
    yield lambda: rwkv_output(m)
    yield lambda: reload_x(m)
    yield lambda: s5_constants(m)
    yield lambda: s5_states(m)
    yield lambda: s5_glu(m)
    yield lambda: pre_norm(m, "mix_again", "norm_mix_pre")
    yield lambda: second_merge(m)
    yield lambda: second_out(m)
    yield lambda: post_norm(m, "mix_post", m.B[1], "norm_mix_post", m.B[2])
    yield lambda: pre_norm(m, "ffn_pre", "norm_ffn_pre")
    yield lambda: ffn_up(m)
    yield lambda: ffn_down(m)
    yield lambda: post_norm(m, "ffn_post", m.B[1], "norm_ffn_post", m.B[2])


def spill_x(m):
    with m.stage() as block:
        @block.scalar
        def _(act):
            act.dma_start(m.dram["x_kept"], m.XT[:, :, :]).then_inc(m.stored, 16)
            m.store_n += 16
            act.wait_ge(m.stored, m.store_n)
        m.issue_weights(block)


def reload_x(m):
    with m.stage() as block:
        @block.scalar
        def _(act):
            act.dma_start(m.XT[:, :, :], m.dram["x_kept"]).then_inc(m.loaded, 16)
            m.load_n += 16
            act.wait_ge(m.loaded, m.load_n)
        m.issue_weights(block)


def second_block(m, stop=None):
    flat = m.memT[:, :, :].rearrange("p a b -> p (a b)")
    four = lambda a: a.rearrange("p s (c v) -> p s c v", c=4)
    m.state = flat[:, 0:1280].rearrange("p (s c v) -> p s c v", s=5, v=64)
    m.pc = m.v2[:, :].rearrange("p (g c) -> p g c", c=4)
    m.gt, m.sbd = four(m.XT[:, 0:4, :]), four(m.XT[:, 4:8, :])
    m.hmat = m.tmp[:, 2:4, :].rearrange("p a (s c v) -> p (a s) c v", s=2, v=64)
    m.w1, m.u1 = four(m.tmp[:, 0:2, :]), four(m.rotary[:, :, :])
    m.rho, m.f_short, m.f_small = (m.s5[:, i, :] for i in range(3))
    for i, stage in enumerate(second_stages(m)):
        if stop is not None and stop[0] == 100 + i:
            store(m, stop[1](m))
            return
        stage()


def store(m, src, name="out"):
    with m.stage() as block:
        @block.scalar
        def _(act):
            act.dma_start(m.dram[name], src).then_inc(m.stored, 16)
            m.store_n += 16
            act.wait_ge(m.stored, m.store_n)
            act.wait_ge(m.pool_dma, m.pool_n)
            for i in range(RING):
                act.wait_ge(m.ring_full[i], 16 * len(range(i, m.issued, RING)))


def program(nc, dram, stop=None):
    with ExitStack() as ctx:
        m = Machine(nc, ctx, dram)
        m.block_expert = m.sb("block_expert", [P, N_BLOCKS], I32)
        m.block_used = m.sb("block_used", [P, N_BLOCKS], I32)
        m.slot = m.sb("slot", [P, 2, TT], I32)
        m.weight = m.sb("weight", [P, 2, TT])
        m.x_in = Alternating([m.sem("x_in0"), m.sem("x_in1")])
        m.y_out = Alternating([m.sem("y_out0"), m.sem("y_out1")])
        load_inputs(m)
        angle_tables(m)
        lam_vectors(m)
        seq = []
        for l in range(DEPTH):
            seq += [(qkv, l), (attention, l), (conv_and_memory_inputs, l),
                    (memory_attention, l), (merge, l), (out_projection, l), (lambda m, l: layer_norm(m, l, 1), l),
                    (route, l), (experts, l), (combine, l), (lambda m, l: layer_norm(m, l, 2), l)]
        for i, (f, l) in enumerate(seq):
            if stop is not None and i == stop[0]:
                store(m, stop[1](m))
                return
            f(m, l)
        if stop is not None and stop[0] == len(seq):
            store(m, stop[1](m))
            return
        second_block(m, stop)
        if stop is None:
            store(m, m.XT[:, :, :])


def _columns(a):
    return np.asarray(a, np.float32).reshape(-1, P).T


def _wide(w):
    return w.reshape(8, P, 512).transpose(1, 0, 2).reshape(P, 4096)


def _tall(w):
    return w.reshape(4, P, 1024).transpose(1, 0, 2).reshape(P, 4096)


def _params(i):
    par = np.zeros((P, PARAMS.total), np.float32)

    def put(name, a):
        lo, hi = PARAMS.at[name]
        par[:, lo:hi] = a
    for l in range(DEPTH):
        put(f"subln{l}", _columns(i["diff_subln_g"][l]))
        put(f"conv_w{l}", _columns(i["conv_w"][l]))
        for n in ("ln1_g", "ln1_b", "ln2_g", "ln2_b"):
            put(f"{n}{l}", _columns(i[n][l]))
    put("router_bias", i["router_bias"][None])
    for n in ("norm_mix_pre", "norm_mix_post", "norm_ffn_pre", "norm_ffn_post", "b_gate"):
        put(n, _columns(i[n + "_2"][0]))
    for n, s in (("shift_mu", "rwkv_shift_mu_2"), ("w0", "rwkv_w0_2"), ("a0", "rwkv_a0_2"), ("k_k", "rwkv_k_k_2"),
                 ("k_a", "rwkv_k_a_2"), ("r_k", "rwkv_r_k_2"), ("lnx_w", "rwkv_lnx_w_2"), ("lnx_b", "rwkv_lnx_b_2"),
                 ("s5_re", "s5_a_re_2"), ("s5_im", "s5_a_im_2"), ("s5_d", "s5_d_2"), ("b_glu", "s5_b_glu_2"),
                 ("ffn_conv_w", "ffn_conv_w_2"), ("ffn_conv_b", "ffn_conv_b_2")):
        put(n, _columns(i[s][0]))
    put("s5_step", _columns(np.repeat(i["s5_log_step_2"][0], 64)))
    return par


def _static_chunks(i):
    out = []
    for kind, l, j in static_names():
        if kind == "in":
            out.append(_wide(i["w_in"][l][:, 512 * j:512 * j + 512]))
        elif kind == "mem_kv":
            out.append(_wide(i["w_mem_kv"][l][:, 512 * j:512 * j + 512]))
        elif kind == "br_attn":
            out.append(_wide(i["w_br_attn"][l][:, 512 * j:512 * j + 512]))
        elif kind in ("br_conv", "br_mem"):
            out.append(_tall(i["w_" + kind][l]))
        elif kind == "out":
            out.append(_wide(i["w_out"][l][:, 512 * j:512 * j + 512]))
        elif kind == "in2":
            w = i["w_in_2"][0]
            w = np.concatenate([w[:, :18 * P], np.zeros((D, 2 * P), np.float32), w[:, 18 * P:]], 1)
            out.append(_wide(w[:, 512 * j:512 * j + 512]))
        elif kind == "br_rwkv":
            out.append(_tall(i["w_branch_rwkv_2"][0]))
        elif kind == "br_s5":
            out.append(_tall(i["w_branch_s5_2"][0]))
        elif kind == "out2":
            out.append(_wide(i["w_out_2"][0][:, 512 * j:512 * j + 512]))
        elif kind == "ffn_up":
            w = i["ffn_w_up_2"][0]
            out.append(_wide(np.concatenate([w[:, 256 * j:256 * j + 256], w[:, D_FF + 256 * j:D_FF + 256 * j + 256]], 1)))
        elif kind == "ffn_down":
            w = i["ffn_w_down_2"][0][512 * j:512 * j + 512]
            out.append(_tall(np.concatenate([w, np.zeros((512 - w.shape[0], D), np.float32)], 0)))
    return np.stack(out)


def _s5_matrices(i):
    b = np.zeros((2, P, 4, P), np.float32)
    c = np.zeros((2, P, 16, 32), np.float32)
    for part, (bn, cn) in enumerate((("s5_b_re_2", "s5_c_re_2"), ("s5_b_im_2", "s5_c_im_2"))):
        bb, cc = np.asarray(i[bn][0]), np.asarray(i[cn][0])
        for g in range(32):
            st, o = g // 2, g % 2
            row = 32 * (st % 4) + 16 * o
            b[part, row:row + 16, st // 4, 64 * o:64 * o + 64] = bb[g].T
            c[part, 64 * o:64 * o + 64, st, 16 * o:16 * o + 16] = cc[g].T
    return np.ascontiguousarray(b.transpose(1, 0, 2, 3)), np.ascontiguousarray(c.transpose(1, 0, 2, 3))


def host_arrays(i):
    i = {k: np.asarray(v) for k, v in i.items()}
    const, rows, small = constants()
    tiles = lambda a: np.ascontiguousarray(a.T.reshape(KT, P, -1).transpose(1, 0, 2))
    s5_b, s5_c = _s5_matrices(i)
    wd = i["w_exp_down"].reshape(DEPTH, E_N, 4, P, D).transpose(0, 1, 3, 2, 4).reshape(DEPTH, E_N, P, 4096)
    up = lambda w: w.reshape(DEPTH, E_N, 8, P, FF_E).transpose(0, 1, 3, 2, 4).reshape(DEPTH, E_N, P, 4096)
    lora = np.zeros((P, 2, 512), np.float32)
    lora[0:64, 0], lora[64:128, 0], lora[:, 1] = i["rwkv_w2_2"][0], i["rwkv_a2_2"][0], i["rwkv_g2_2"][0]
    return {
        "xT": tiles(i["x"][0]), "memT": tiles(i["mem"][0]),
        "positions": np.ascontiguousarray(np.broadcast_to(i["positions"], (P, SEQ)).astype(np.int32)),
        "lambdas": np.ascontiguousarray(np.broadcast_to(
            np.stack([i[f"lambda_{n}"] for n in ("q1", "k1", "q2", "k2")], 1).reshape(-1), (P, DEPTH * 4 * 64))),
        "consts": const, "rows": rows, "small": small, "params": _params(i),
        "w_router": np.ascontiguousarray(i["w_router"].reshape(KT, P, E_N).transpose(1, 0, 2)),
        "w_static": _static_chunks(i),
        "w_expert": np.stack([up(i["w_exp_gate"]), up(i["w_exp_up"]), wd], 2).reshape(-1, P, 4096),
        "s5_b": s5_b, "s5_c": s5_c, "lora": lora,
        "w_glu": np.ascontiguousarray(i["s5_w_glu_2"][0].reshape(4, P, 512).transpose(1, 0, 2)),
    }


def kernel(**inputs):
    import concourse.bacc as _bacc
    from concourse.bass_utils import run_bass_kernel_spmd as _run

    nc = _bacc.Bacc("TRN2", target_bir_lowering=False, num_devices=1)
    arrays = {f"in_{k}": v for k, v in host_arrays(inputs).items()}
    dram = {k[3:]: nc.dram_tensor(k, v.shape, mybir.dt.from_np(v.dtype), kind="ExternalInput").ap()
            for k, v in arrays.items()}
    dram["slots_x"] = nc.dram_tensor("slots_x", (N_BLOCKS * P, D), F32, kind="Internal").ap()
    dram["slots_y"] = nc.dram_tensor("slots_y", (N_BLOCKS * P, D), F32, kind="Internal").ap()
    dram["x_kept"] = nc.dram_tensor("x_kept", (P, KT, SEQ), F32, kind="Internal").ap()
    dram["out"] = nc.dram_tensor("out_xT", (P, KT, SEQ), F32, kind="ExternalOutput").ap()
    program(nc, dram)
    r = _run(nc, [arrays], core_ids=[0])
    got = np.asarray(r.results[0]["out_xT"])
    return np.ascontiguousarray(got.transpose(2, 1, 0).reshape(1, SEQ, D))
```
